# Optimizing a Trainium2 kernel written in Bass

```python
import numpy as np
import jax, jax.numpy as jnp
from jax import lax

D_MODEL = 1024
BATCH = 1
SEQ = 2048
DEPTH = 1

HEAD_DIM = 64
NSA_HEADS = 8
NSA_KV_GROUPS = 2
NSA_GROUP_SIZE = NSA_HEADS // NSA_KV_GROUPS
CMP_BLOCK = 32
CMP_STRIDE = 16
CMP_HIDDEN = 128
SEL_BLOCK = 64
SEL_TOPK = 8
WINDOW = 512
NSA_Q_BLOCK = 64
FORCED_SCORE = 1e9
DIFF_HEADS = 4
DIFF_Q_BLOCK = 128
MOE_GROUPS = 4
EXPERTS_PER_GROUP = 4
N_EXPERTS = MOE_GROUPS * EXPERTS_PER_GROUP
MOE_TOPK = 2
EXPERT_FF = D_MODEL // 8

RMS_EPS = 1e-6
SUBLN_EPS = 1e-5
NEG_INF = -1e30
N_ALIBI_HEADS = NSA_HEADS + DIFF_HEADS

NSA_Q_COLS = NSA_HEADS * HEAD_DIM
NSA_KV_COLS = NSA_KV_GROUPS * HEAD_DIM
NSA_GATE_COLS = 3 * NSA_HEADS
DIFF_QK_COLS = DIFF_HEADS * 2 * HEAD_DIM
DIFF_V_COLS = DIFF_HEADS * 2 * HEAD_DIM
IN_COLS = NSA_Q_COLS + 6 * NSA_KV_COLS + NSA_GATE_COLS + 2 * DIFF_QK_COLS + DIFF_V_COLS + 2 * D_MODEL

kernel_name = 'hybrid_nsa_diffattn_hier_moe'

def rms_norm(x, g, eps=RMS_EPS):
    xf = x.astype(jnp.float32)
    y = xf * lax.rsqrt(jnp.mean(xf * xf, axis=-1, keepdims=True) + eps)
    return (y * g.astype(jnp.float32)).astype(x.dtype)

def alibi_slopes():
    s = 2.0 ** (-8.0 * np.arange(1, N_ALIBI_HEADS + 1) / N_ALIBI_HEADS)
    return jnp.asarray(s, dtype=jnp.float32)

def masked_softmax(s, mask):
    return jax.nn.softmax(jnp.where(mask, s, NEG_INF), axis=-1)

def split_points():
    sizes = [NSA_Q_COLS] + [NSA_KV_COLS] * 6 + [NSA_GATE_COLS, DIFF_QK_COLS, DIFF_QK_COLS, DIFF_V_COLS, D_MODEL, D_MODEL]
    return [int(v) for v in np.cumsum(sizes)[:-1]]

def compress_tokens(kv, pe, w1, b1, w2, b2):
    B, T, G, HD = kv.shape
    nc = (T - CMP_BLOCK) // CMP_STRIDE + 1
    idx = np.arange(nc)[:, None] * CMP_STRIDE + np.arange(CMP_BLOCK)[None, :]
    blk = kv[:, idx] + pe[:, None, :]
    blk = jnp.swapaxes(blk, 2, 3).reshape(B, nc, G, CMP_BLOCK * HD)
    h = jax.nn.gelu(blk @ w1 + b1)
    return h @ w2 + b2

def cmp_to_sel_matrix(nc, nb):
    c0 = np.arange(nc)[:, None] * CMP_STRIDE
    s0 = np.arange(nb)[None, :] * SEL_BLOCK
    ov = np.maximum(0, np.minimum(c0 + CMP_BLOCK, s0 + SEL_BLOCK) - np.maximum(c0, s0))
    return jnp.asarray(ov / CMP_BLOCK, dtype=jnp.float32)

def nsa_attention(q, kc, vc, ks, vs, kw, vw, gate_logits, slopes):
    B, T = q.shape[0], q.shape[1]
    dt = q.dtype
    G, Hg, HD, QB = NSA_KV_GROUPS, NSA_GROUP_SIZE, HEAD_DIM, NSA_Q_BLOCK
    nc = kc.shape[1]
    nb = T // SEL_BLOCK
    k_sel = min(SEL_TOPK, nb)
    n_chunks = T // QB
    scale = HD ** -0.5
    sl = slopes.reshape(G, Hg)[None, :, :, None, None]
    cmp_end = jnp.arange(nc) * CMP_STRIDE + CMP_BLOCK - 1
    a_sel = cmp_to_sel_matrix(nc, nb)
    blk_start = jnp.arange(nb) * SEL_BLOCK
    blk_ids = jnp.arange(nb)
    ks_b = ks.reshape(B, nb, SEL_BLOCK, G, HD).transpose(0, 3, 1, 2, 4)
    vs_b = vs.reshape(B, nb, SEL_BLOCK, G, HD).transpose(0, 3, 1, 2, 4)
    kw_p = jnp.pad(kw, ((0, 0), (WINDOW, 0), (0, 0), (0, 0)))
    vw_p = jnp.pad(vw, ((0, 0), (WINDOW, 0), (0, 0), (0, 0)))
    bi = jnp.arange(B)[:, None, None, None]
    gi = jnp.arange(G)[None, :, None, None]
    qs = q.reshape(B, n_chunks, QB, G, Hg, HD).swapaxes(0, 1)
    gs = jax.nn.sigmoid(gate_logits.astype(jnp.float32)).astype(dt)
    gs = gs.reshape(B, n_chunks, QB, G, Hg, 3).swapaxes(0, 1)
    starts = jnp.arange(n_chunks, dtype=jnp.int32) * QB

    def chunk(args):
        qc, gc, start = args
        t = start + jnp.arange(QB)
        s = jnp.einsum('bqghd,bngd->bghqn', qc, kc).astype(jnp.float32) * scale
        dist = (t[:, None] - cmp_end[None, :]).astype(jnp.float32)
        valid = cmp_end[None, :] <= t[:, None]
        p_cmp = masked_softmax(s - sl * dist, valid) * jnp.any(valid, axis=-1)[:, None].astype(jnp.float32)
        o_cmp = jnp.einsum('bghqn,bngd->bqghd', p_cmp.astype(dt), vc)
        imp = jnp.einsum('bghqn,nm->bgqm', p_cmp, a_sel)
        cur = t // SEL_BLOCK
        forced = (blk_ids[None, :] == 0) | (blk_ids[None, :] == cur[:, None]) | (blk_ids[None, :] == cur[:, None] - 1)
        imp = jnp.where(forced, FORCED_SCORE, imp)
        imp = jnp.where(blk_start[None, :] <= t[:, None], imp, -1.0)
        _, idx = lax.top_k(imp, k_sel)
        kg = ks_b[bi, gi, idx].reshape(B, G, QB, k_sel * SEL_BLOCK, HD)
        vg = vs_b[bi, gi, idx].reshape(B, G, QB, k_sel * SEL_BLOCK, HD)
        tok = (idx[..., None] * SEL_BLOCK + jnp.arange(SEL_BLOCK)).reshape(B, G, QB, k_sel * SEL_BLOCK)
        s = jnp.einsum('bqghd,bgqld->bghql', qc, kg).astype(jnp.float32) * scale
        dist = (t[:, None] - tok).astype(jnp.float32)[:, :, None]
        p_sel = masked_softmax(s - sl * dist, (tok <= t[:, None])[:, :, None])
        o_sel = jnp.einsum('bghql,bgqld->bqghd', p_sel.astype(dt), vg)
        kwc = lax.dynamic_slice_in_dim(kw_p, start, QB + WINDOW, axis=1)
        vwc = lax.dynamic_slice_in_dim(vw_p, start, QB + WINDOW, axis=1)
        kpos = start - WINDOW + jnp.arange(QB + WINDOW)
        s = jnp.einsum('bqghd,bkgd->bghqk', qc, kwc).astype(jnp.float32) * scale
        d_i = t[:, None] - kpos[None, :]
        valid = (d_i >= 0) & (d_i < WINDOW) & (kpos[None, :] >= 0)
        p_win = masked_softmax(s - sl * d_i.astype(jnp.float32), valid)
        o_win = jnp.einsum('bghqk,bkgd->bqghd', p_win.astype(dt), vwc)
        return gc[..., 0:1] * o_cmp + gc[..., 1:2] * o_sel + gc[..., 2:3] * o_win

    out = lax.map(chunk, (qs, gs, starts))
    return out.swapaxes(0, 1).reshape(B, T, NSA_HEADS * HEAD_DIM)

def diff_attention(q, k, v, lam, lam_init, subln_g, slopes):
    B, T = q.shape[0], q.shape[1]
    dt = q.dtype
    QB = DIFF_Q_BLOCK
    n_chunks = T // QB
    scale = HEAD_DIM ** -0.5
    sl = slopes[None, :, None, None, None]
    kpos = jnp.arange(T)
    qs = q.reshape(B, n_chunks, QB, DIFF_HEADS, 2, HEAD_DIM).swapaxes(0, 1)
    starts = jnp.arange(n_chunks, dtype=jnp.int32) * QB

    def chunk(args):
        qc, start = args
        t = start + jnp.arange(QB)
        s = jnp.einsum('bqhcd,bkhcd->bhcqk', qc, k).astype(jnp.float32) * scale
        d_i = t[:, None] - kpos[None, :]
        p = masked_softmax(s - sl * d_i.astype(jnp.float32), d_i >= 0)
        a = p[:, :, 0] - lam * p[:, :, 1]
        return jnp.einsum('bhqk,bkhe->bqhe', a.astype(dt), v)

    o = lax.map(chunk, (qs, starts)).swapaxes(0, 1).reshape(B, T, DIFF_HEADS, 2 * HEAD_DIM)
    o = rms_norm(o, subln_g, SUBLN_EPS) * (1.0 - lam_init)
    return o.reshape(B, T, DIFF_HEADS * 2 * HEAD_DIM)

def hier_moe(x, wg, bg, we, be, w_gate, w_up, w_down):
    B, T, D = x.shape
    dt = x.dtype
    xf = x.reshape(B * T, D)
    g_logits = (xf @ wg).astype(jnp.float32) + bg.astype(jnp.float32)
    g_prob = jax.nn.softmax(g_logits, axis=-1)
    g_idx = jnp.argmax(g_logits, axis=-1)
    g_w = jnp.take_along_axis(g_prob, g_idx[:, None], axis=1)
    e_logits = jnp.einsum('nd,dge->nge', xf, we).astype(jnp.float32) + be.astype(jnp.float32)
    e_logits = jnp.take_along_axis(e_logits, g_idx[:, None, None], axis=1)[:, 0]
    top_v, top_i = lax.top_k(e_logits, MOE_TOPK)
    top_w = jax.nn.softmax(top_v, axis=-1) * g_w
    combine = jnp.einsum('ng,nke->nge', jax.nn.one_hot(g_idx, MOE_GROUPS),
                         jax.nn.one_hot(top_i, EXPERTS_PER_GROUP) * top_w[..., None])
    combine = combine.reshape(B * T, N_EXPERTS).astype(dt)
    h = jax.nn.silu(jnp.einsum('nd,edf->nef', xf, w_gate)) * jnp.einsum('nd,edf->nef', xf, w_up)
    y = jnp.einsum('nef,efd->nd', h * combine[:, :, None], w_down)
    return y.reshape(B, T, D)

def setup_inputs(seed: int = 0) -> dict:
    key = jax.random.key(seed)
    ks = jax.random.split(key, 24)
    D, L, HD = D_MODEL, DEPTH, HEAD_DIM

    def nrm(k, shape, scale):
        return jax.random.normal(k, shape, jnp.float32) * scale

    def gain(k, shape):
        return 1.0 + 0.02 * jax.random.normal(k, shape, jnp.float32)

    return {
        'x': nrm(ks[0], (BATCH, SEQ, D), 1.0),
        'norm1_g': gain(ks[1], (L, D)),
        'w_in': nrm(ks[2], (L, D, IN_COLS), D ** -0.5),
        'cmp_pe': nrm(ks[3], (L, 2, CMP_BLOCK, HD), 0.02),
        'cmp_w1': nrm(ks[4], (L, 2, CMP_BLOCK * HD, CMP_HIDDEN), (CMP_BLOCK * HD) ** -0.5),
        'cmp_b1': nrm(ks[5], (L, 2, CMP_HIDDEN), 0.02),
        'cmp_w2': nrm(ks[6], (L, 2, CMP_HIDDEN, HD), CMP_HIDDEN ** -0.5),
        'cmp_b2': nrm(ks[7], (L, 2, HD), 0.02),
        'diff_lambda': nrm(ks[8], (L, 4, HD), 0.1),
        'diff_subln_g': gain(ks[9], (L, 2 * HD)),
        'w_branch_a': nrm(ks[10], (L, NSA_HEADS * HD, D), (NSA_HEADS * HD) ** -0.5),
        'w_branch_b': nrm(ks[11], (L, DIFF_HEADS * 2 * HD, D), (DIFF_HEADS * 2 * HD) ** -0.5),
        'w_out': nrm(ks[12], (L, D, D), D ** -0.5),
        'norm2_g': gain(ks[13], (L, D)),
        'router_grp_w': nrm(ks[14], (L, D, MOE_GROUPS), D ** -0.5),
        'router_grp_b': nrm(ks[15], (L, MOE_GROUPS), 0.01),
        'router_exp_w': nrm(ks[16], (L, D, MOE_GROUPS, EXPERTS_PER_GROUP), D ** -0.5),
        'router_exp_b': nrm(ks[17], (L, MOE_GROUPS, EXPERTS_PER_GROUP), 0.01),
        'exp_w_gate': nrm(ks[18], (L, N_EXPERTS, D, EXPERT_FF), D ** -0.5),
        'exp_w_up': nrm(ks[19], (L, N_EXPERTS, D, EXPERT_FF), D ** -0.5),
        'exp_w_down': nrm(ks[20], (L, N_EXPERTS, EXPERT_FF, D), EXPERT_FF ** -0.5),
        'final_norm_g': gain(ks[21], (D,)),
    }

def reference(x, norm1_g, w_in, cmp_pe, cmp_w1, cmp_b1, cmp_w2, cmp_b2, diff_lambda, diff_subln_g,
              w_branch_a, w_branch_b, w_out, norm2_g, router_grp_w, router_grp_b, router_exp_w,
              router_exp_b, exp_w_gate, exp_w_up, exp_w_down, final_norm_g):
    B, T, _ = x.shape
    slopes = alibi_slopes()
    sl_nsa, sl_diff = slopes[:NSA_HEADS], slopes[NSA_HEADS:]
    cuts = split_points()
    G, HD = NSA_KV_GROUPS, HEAD_DIM
    h = x
    for l in range(DEPTH):
        xn = rms_norm(h, norm1_g[l])
        proj = xn @ w_in[l]
        (nq, kc_r, vc_r, ks_r, vs_r, kw_r, vw_r, ngate, dq, dk, dv, gate_a, gate_b) = jnp.split(proj, cuts, axis=-1)
        kc = compress_tokens(kc_r.reshape(B, T, G, HD), cmp_pe[l, 0], cmp_w1[l, 0], cmp_b1[l, 0], cmp_w2[l, 0], cmp_b2[l, 0])
        vc = compress_tokens(vc_r.reshape(B, T, G, HD), cmp_pe[l, 1], cmp_w1[l, 1], cmp_b1[l, 1], cmp_w2[l, 1], cmp_b2[l, 1])
        y_a = nsa_attention(nq.reshape(B, T, NSA_HEADS, HD), kc, vc,
                            ks_r.reshape(B, T, G, HD), vs_r.reshape(B, T, G, HD),
                            kw_r.reshape(B, T, G, HD), vw_r.reshape(B, T, G, HD),
                            ngate.reshape(B, T, NSA_HEADS, 3), sl_nsa)
        lam_init = 0.8 - 0.6 * float(np.exp(-0.3 * l))
        lp = diff_lambda[l].astype(jnp.float32)
        lam = jnp.exp(jnp.sum(lp[0] * lp[1])) - jnp.exp(jnp.sum(lp[2] * lp[3])) + lam_init
        y_b = diff_attention(dq.reshape(B, T, DIFF_HEADS, 2, HD), dk.reshape(B, T, DIFF_HEADS, 2, HD),
                             dv.reshape(B, T, DIFF_HEADS, 2 * HD), lam, lam_init, diff_subln_g[l], sl_diff)
        merged = jax.nn.sigmoid(gate_a) * (y_a @ w_branch_a[l]) + jax.nn.sigmoid(gate_b) * (y_b @ w_branch_b[l])
        h = h + merged @ w_out[l]
        h = h + hier_moe(rms_norm(h, norm2_g[l]), router_grp_w[l], router_grp_b[l], router_exp_w[l],
                         router_exp_b[l], exp_w_gate[l], exp_w_up[l], exp_w_down[l])
    return rms_norm(h, final_norm_g)


_drawn_inputs = setup_inputs


def setup_inputs(seed=0):
    import zlib

    import numpy as np

    out = dict(_drawn_inputs(seed))
    spreads = {}
    factors = {'cmp_pe': 22.096,
     'cmp_b1': 8.0,
     'cmp_b2': 5.906,
     'diff_subln_g': 3.529,
     'router_grp_b': 64.0,
     'router_exp_b': 21.008,
     'final_norm_g': 7.514,
     'norm2_g': 3.836}
    for name, (base, spread) in spreads.items():
        noise = np.random.default_rng([zlib.crc32(name.encode()), seed]).standard_normal(out[name].shape)
        drawn = base * np.exp(spread * noise) if base else spread * noise
        out[name] = __import__('jax').numpy.asarray(drawn.astype(out[name].dtype))
    for name, factor in factors.items():
        out[name] = (out[name] * factor).astype(out[name].dtype)
    return out
```

```python
from contextlib import contextmanager

import numpy as np

D = 1024
T = 2048
P = 128
HD = 64
DT = D // P
NT = T // P
NCH = T // 512
NSA_HEADS, GROUPS, PAIRS = 8, 2, 4
DIFF_HEADS = 4
N_ALIBI = NSA_HEADS + DIFF_HEADS
CMP_BLOCK, CMP_STRIDE, CMP_HIDDEN = 32, 16, 128
NCMP = (T - CMP_BLOCK) // CMP_STRIDE + 1
SEL_BLOCK, SEL_TOPK, WINDOW = 64, 8, 512
NBLK = T // SEL_BLOCK
NG, NE, FF = 4, 4, 128
NSLOT = (NT + NG) * P
ROW = 8
RMS_EPS, SUBLN_EPS = 1e-6, 1e-5
NEG = -1e30
FORCED = 1e9
LAM_INIT = 0.8 - 0.6 * float(np.exp(-0.3 * 0))
V_SEL, V_WIN, V_GATE, V_DIFF = 0, 128, 256, 280
VCOLS = 280 + 512
T_Q, T_KC, T_VC, T_KS, T_KW, T_DIFF, T_GATE = 0, 4, 5, 6, 7, 8, 16


@contextmanager
def phase_semaphores(nc):
    taken = []

    def named(name):
        taken.append(nc.alloc_semaphore(name))
        return taken[-1]

    yield named
    clear_semaphores(nc, taken)
    for x in taken:
        nc.release_semaphore(x)


def clear_semaphores(nc, sems):
    for x in sems:
        nc.gpsimd.sem_clear(x)
    nc.all_engine_barrier()


def norm_and_v_projection(nc, x_d, wv_d, g_d, ident, half, xnT, vsw, vd):
    import concourse.bass as bass
    from concourse import mybir
    from contextlib import ExitStack

    fp32 = mybir.dt.float32
    ALU = mybir.AluOpType
    ACT = mybir.ActivationFunctionType
    with ExitStack() as ctx:
        sem = ctx.enter_context(phase_semaphores(nc))
        xin = ctx.enter_context(nc.sbuf_tensor("p1_xin", [P, 2, D], fp32))
        sq = ctx.enter_context(nc.sbuf_tensor("p1_sq", [P, D], fp32))
        xs = ctx.enter_context(nc.sbuf_tensor("p1_xs", [P, 2, D], fp32))
        xt = ctx.enter_context(nc.sbuf_tensor("p1_xt", [P, 2, DT, P], fp32))
        wv = ctx.enter_context(nc.sbuf_tensor("p1_wv", [P, DT, VCOLS], fp32))
        gain = ctx.enter_context(nc.sbuf_tensor("p1_gain", [P, DT], fp32))
        stat = ctx.enter_context(nc.sbuf_tensor("p1_stat", [P, 2, 4], fp32))
        tr = [ctx.enter_context(nc.psum_tensor(f"p1_tr{k}", [P, 4, P], fp32)) for k in range(2)]
        pv = [[ctx.enter_context(nc.psum_tensor(f"p1_pv{b}{k}", [P, 512], fp32)) for k in range(2)] for b in range(2)]
        x_in = [sem(f"p1_x_in{b}") for b in range(2)]
        w_in = sem("p1_w_in")
        c_in = sem("p1_c_in")
        dve_step = sem("p1_dve_step")
        var_ready = sem("p1_var_ready")
        rstd_ready = sem("p1_rstd_ready")
        xs_ready = sem("p1_xs_ready")
        tr_ready = sem("p1_tr_ready")
        xt_ready = sem("p1_xt_ready")
        pv_ready = sem("p1_pv_ready")
        pv_free = sem("p1_pv_free")
        xt_copied = sem("p1_xt_copied")
        sp_step = sem("p1_sp_step")
        x_t = x_d.rearrange("(n p) d -> n p d", p=P)
        block = ctx.enter_context(nc.Block())

        @block.sync
        def _(sp):
            sp.dma_start(xin[:, 0, :], x_t[0]).then_inc(x_in[0], 16)
            sp.dma_start(gain[:], g_d).then_inc(c_in, 16)
            sp.dma_start(xin[:, 1, :], x_t[1]).then_inc(x_in[1], 16)
            for dt in range(DT):
                sp.dma_start(wv[:, dt, :], wv_d[:, dt, :]).then_inc(w_in, 16)
            with sp.Fori(0, NT // 2 - 1) as i:
                for b in range(2):
                    sp.wait_ge(xs_ready, 2 * i + b + 1)
                    sp.sem_inc(sp_step, 1)
                    sp.dma_start(xin[:, b, :], x_t[2 * i + b + 2]).then_inc(x_in[b], 16)

        @block.gpsimd
        def _(pool):
            with pool.Fori(0, NT // 2) as i:
                for b in range(2):
                    pool.wait_ge(var_ready, 2 * i + b + 1)
                    pool.sem_inc(sp_step, 1)
                    nc.gpsimd.tensor_tensor(stat[:, b, 2:3], stat[:, b, 1:2], half[:, 0:1], ALU.pow).then_inc(rstd_ready, 1)

        @block.vector
        def _(dve):
            def scale(i, b):
                dve.wait_ge(x_in[b], 16 * i + 16)
                dve.sem_inc(sp_step, 1)
                nc.vector.tensor_tensor_reduce(out=sq[:], in0=xin[:, b, :], in1=xin[:, b, :], scale=1.0, scalar=0.0,
                                               op0=ALU.mult, op1=ALU.add, accum_out=stat[:, b, 0:1]).then_inc(dve_step, 1)
                dve.wait_ge(dve_step, 2 * i + b + 1)
                nc.vector.tensor_scalar(stat[:, b, 1:2], stat[:, b, 0:1], 1.0 / D, RMS_EPS, ALU.mult, ALU.add).then_inc(var_ready, 1)
                dve.wait_ge(rstd_ready, 2 * i + b + 1)
                nc.vector.tensor_scalar(xs[:, b, :], xin[:, b, :], stat[:, b, 2:3], None, ALU.mult).then_inc(xs_ready, 1)

            def apply_gain(i, b):
                dve.wait_ge(tr_ready, 2 * i + b + 1)
                dve.wait_ge(xt_copied, 2 * i + b + 1)
                for k in range(2):
                    nc.vector.tensor_tensor(xt[:, b, 4 * k:4 * k + 4, :], tr[k][:],
                                            gain[:, 4 * k:4 * k + 4].unsqueeze(2).to_broadcast([P, 4, P]),
                                            ALU.mult).then_inc(xt_ready, 1)

            dve.wait_ge(c_in, 16)
            scale(0, 0)
            with dve.Fori(0, NT // 2 - 1) as i:
                scale(i, 1)
                apply_gain(i, 0)
                scale(i + 1, 0)
                apply_gain(i, 1)
            scale(NT // 2 - 1, 1)
            apply_gain(NT // 2 - 1, 0)
            apply_gain(NT // 2 - 1, 1)

        @block.scalar
        def _(act):
            act.sem_inc(pv_free, 2)
            act.sem_inc(xt_copied, 2)
            with act.Fori(0, NT // 2) as i:
                for b in range(2):
                    n = 2 * i + b
                    act.wait_ge(xt_ready, 2 * n + 2)
                    nc.scalar.activation(xnT[:, :, bass.ts(n, P)], xt[:, b, :, :], ACT.Copy).then_inc(xt_copied, 1)
                    act.wait_ge(pv_ready, n + 1)
                    nc.scalar.activation(vsw[:, n, :], pv[b][0][:, 0:V_DIFF], ACT.Copy)
                    nc.scalar.activation(vd[:, n, :], pv[b][1][:, :], ACT.Copy).then_inc(pv_free, 1)

        @block.tensor
        def _(pe):
            def turn(i, b):
                pe.wait_ge(xs_ready, 2 * i + b + 1)
                for dt in range(DT):
                    mm = nc.tensor.transpose(tr[dt // 4][:, dt % 4, :], xs[:, b, dt * P:(dt + 1) * P], ident[:])
                mm.then_inc(tr_ready, 1)

            def emptied(i, b):
                pe.wait_ge(xt_ready, 4 * i + 2 * b + 2)

            def project(i, b):
                pe.wait_ge(pv_free, 2 * i + b + 1)
                pe.wait_ge(w_in, 16 * DT)
                for dt in range(DT):
                    nc.tensor.matmul(pv[b][0][:, 0:V_DIFF], xt[:, b, dt, :], wv[:, dt, 0:V_DIFF], start=(dt == 0), stop=(dt == DT - 1))
                    mm = nc.tensor.matmul(pv[b][1][:, :], xt[:, b, dt, :], wv[:, dt, V_DIFF:VCOLS], start=(dt == 0), stop=(dt == DT - 1))
                mm.then_inc(pv_ready, 1)

            pe.wait_ge(c_in, 16)
            turn(0, 0)
            with pe.Fori(0, NT // 2 - 1) as i:
                emptied(i, 0)
                turn(i, 1)
                project(i, 0)
                emptied(i, 1)
                turn(i + 1, 0)
                project(i, 1)
            emptied(NT // 2 - 1, 0)
            turn(NT // 2 - 1, 1)
            project(NT // 2 - 1, 0)
            emptied(NT // 2 - 1, 1)
            project(NT // 2 - 1, 1)


def t_projection(nc, wt_d, xnT, qkT_d, spills):
    from concourse import mybir
    from contextlib import ExitStack

    fp32 = mybir.dt.float32
    ACT = mybir.ActivationFunctionType
    with ExitStack() as ctx:
        sem = ctx.enter_context(phase_semaphores(nc))
        w = ctx.enter_context(nc.sbuf_tensor("p2_w", [P, 2, DT, P], fp32))
        stage = ctx.enter_context(nc.sbuf_tensor("p2_stage", [P, 2, T], fp32))
        ps = [[ctx.enter_context(nc.psum_tensor(f"p2_ps{b}{c}", [P, 512], fp32)) for c in range(NCH)] for b in range(2)]
        w_in = [sem(f"p2_w_in{b}") for b in range(2)]
        ps_ready = sem("p2_ps_ready")
        act_done = sem("p2_act_done")
        dve_done = sem("p2_dve_done")
        stored = [sem(f"p2_stored{b}") for b in range(2)]
        spilled = sem("p2_spilled")
        sp_step = sem("p2_sp_step")
        block = ctx.enter_context(nc.Block())

        @block.sync
        def _(sp):
            for b in range(2):
                sp.sem_inc(stored[b], 16)
                sp.dma_start(w[:, b, :, :], wt_d[b]).then_inc(w_in[b], 16)
            for to, of in spills:
                sp.dma_start(to, of).then_inc(spilled, 16)
            with sp.Fori(0, T_GATE // 2) as i:
                for b in range(2):
                    sp.wait_ge(ps_ready, 8 * i + 4 * b + 4)
                    sp.sem_inc(sp_step, 1)
                    sp.dma_start(w[:, b, :, :], wt_d[2 * i + b + 2]).then_inc(w_in[b], 16)
                    sp.wait_ge(act_done, 4 * i + 2 * b + 6)
                    sp.sem_inc(sp_step, 1)
                    sp.wait_ge(dve_done, 4 * i + 2 * b + 6)
                    sp.sem_inc(sp_step, 1)
                    sp.dma_start(qkT_d[2 * i + b], stage[:, b, :]).then_inc(stored[b], 16)
            for b in range(2):
                sp.wait_ge(stored[b], 16 * (T_GATE // 2 + 1))
                sp.wait_ge(w_in[b], 16 * (T_GATE // 2 + 1))
            sp.wait_ge(spilled, 16 * len(spills))

        @block.tensor
        def _(pe):
            with pe.Fori(0, T_GATE // 2) as i:
                for b in range(2):
                    pe.wait_ge(w_in[b], 16 * i + 16)
                    pe.wait_ge(act_done, 4 * i + 2 * b + 2)
                    pe.wait_ge(dve_done, 4 * i + 2 * b + 2)
                    for c in range(NCH):
                        for dt in range(DT):
                            mm = nc.tensor.matmul(ps[b][c][:], w[:, b, dt, :], xnT[:, dt, c * 512:(c + 1) * 512],
                                                  start=(dt == 0), stop=(dt == DT - 1))
                        mm.then_inc(ps_ready, 1)

        def evacuate(eng, copy, done, first):
            eng.sem_inc(done, 4)
            with eng.Fori(0, T_GATE // 2) as i:
                for b in range(2):
                    eng.wait_ge(stored[b], 16 * i + 16)
                    for c in range(first, NCH, 2):
                        eng.wait_ge(ps_ready, 8 * i + 4 * b + c + 1)
                        copy(stage[:, b, c * 512:(c + 1) * 512], ps[b][c][:]).then_inc(done, 1)

        @block.scalar
        def _(act):
            evacuate(act, lambda o, s: nc.scalar.activation(o, s, ACT.Copy), act_done, 0)

        @block.vector
        def _(dve):
            evacuate(dve, lambda o, s: nc.vector.tensor_copy(o, s), dve_done, 1)


def compress(nc, d, s):
    from concourse import mybir
    from contextlib import ExitStack

    fp32 = mybir.dt.float32
    ALU = mybir.AluOpType
    ACT = mybir.ActivationFunctionType
    NJ = CMP_BLOCK // 2
    span = CMP_STRIDE * (NCMP - 1) + 1
    with ExitStack() as ctx:
        raw = [[ctx.enter_context(nc.sbuf_tensor(f"c_raw{v}{g}", [P, T], fp32)) for g in range(GROUPS)] for v in range(2)]
        w1 = [ctx.enter_context(nc.sbuf_tensor(f"c_w1{v}", [P, NJ, CMP_HIDDEN], fp32)) for v in range(2)]
        pe_sb = ctx.enter_context(nc.sbuf_tensor("c_pe", [P, 2, NJ], fp32))
        b1 = ctx.enter_context(nc.sbuf_tensor("c_b1", [P, 2], fp32))
        w2 = ctx.enter_context(nc.sbuf_tensor("c_w2", [P, 2, P], fp32))
        w2v = ctx.enter_context(nc.sbuf_tensor("c_w2v", [P, HD], fp32))
        b2k = ctx.enter_context(nc.sbuf_tensor("c_b2k", [P, 1], fp32))
        b2v = ctx.enter_context(nc.sbuf_tensor("c_b2v", [P, P], fp32))
        bias = ctx.enter_context(nc.sbuf_tensor("c_bias", [P, 2], fp32))
        hid = ctx.enter_context(nc.sbuf_tensor("c_hid", [P, 4, P], fp32))
        ph = [ctx.enter_context(nc.psum_tensor(f"c_ph{k}", [P, 512], fp32)) for k in range(4)]
        pb = ctx.enter_context(nc.psum_tensor("c_pb", [P, 512], fp32))
        pk = ctx.enter_context(nc.psum_tensor("c_pk", [P, 512], fp32))
        pv = ctx.enter_context(nc.psum_tensor("c_pv", [P, 512], fp32))
        kept_in = nc.alloc_semaphore("c_kept_in")
        vsw_in = nc.alloc_semaphore("c_vsw_in")
        cleared = nc.alloc_semaphore("c_cleared")
        k_in = nc.alloc_semaphore("c_k_in")
        v_in = nc.alloc_semaphore("c_v_in")
        small_in = nc.alloc_semaphore("c_small_in")
        pb_ready = nc.alloc_semaphore("c_pb_ready")
        bias_ready = nc.alloc_semaphore("c_bias_ready")
        ph_ready = nc.alloc_semaphore("c_ph_ready")
        hid_zero = nc.alloc_semaphore("c_hid_zero")
        hid_ready = nc.alloc_semaphore("c_hid_ready")
        pkv_ready = nc.alloc_semaphore("c_pkv_ready")
        block = ctx.enter_context(nc.Block())

        @block.sync
        def _(sp):
            for o, i in ((pe_sb[:], d["cmp_pe"]), (b1[:], d["cmp_b1"]), (w2[:], d["cmp_w2k"]), (w2v[:], d["cmp_w2v"]),
                         (b2k[:], d["cmp_b2k"]), (b2v[:], d["cmp_b2v"])):
                sp.dma_start(o, i).then_inc(small_in, 16)
            for v, got in ((0, k_in), (1, v_in)):
                if v == 1:
                    sp.wait_ge(k_in, 16 * 5)
                sp.dma_start(w1[v][:], d["cmp_w1"][v]).then_inc(got, 16)
                for g in range(GROUPS):
                    rows = slice(g * HD, (g + 1) * HD)
                    sp.dma_start(raw[v][g][0:HD, :], d["qkT"][T_KC + v][rows, :]).then_inc(got, 16)
                    sp.dma_start(raw[v][g][HD:P, 0:T - 1], d["qkT"][T_KC + v][rows, 1:T]).then_inc(got, 16)
            sp.dma_start(s.vsw[:], d["vsw"]).then_inc(vsw_in, 16)
            for g in range(GROUPS):
                own, other = slice(g * HD, (g + 1) * HD), slice((1 - g) * HD, (2 - g) * HD)
                sp.dma_start(s.ks[g][own, :], d["qkT"][T_KS][own, :]).then_inc(kept_in, 16)
                sp.dma_start(s.ks[g][other, :], d["blk_ind"]).then_inc(kept_in, 16)
                sp.dma_start(s.kw[g][own, :], d["qkT"][T_KW][own, :]).then_inc(kept_in, 16)
            sp.wait_ge(kept_in, 16 * 6)

        @block.gpsimd
        def _(pool):
            nc.gpsimd.memset(s.pbar[:], 0.0)

        @block.tensor
        def _(pe):
            pe.wait_ge(small_in, 16 * 6)
            for v, got in ((0, k_in), (1, v_in)):
                pe.wait_ge(got, 16 * 5)
                for j in range(NJ):
                    mm = nc.tensor.matmul(pb[:, v:v + 1], w1[v][:, j, :], pe_sb[:, v, j:j + 1], start=(j == 0), stop=(j == NJ - 1))
                mm.then_inc(pb_ready, 1)
                for g in range(GROUPS):
                    for j in range(NJ):
                        mm = nc.tensor.matmul(ph[2 * v + g][:, 0:NCMP], w1[v][:, j, :], raw[v][g][:, 2 * j:2 * j + span:CMP_STRIDE],
                                              start=(j == 0), stop=(j == NJ - 1))
                    mm.then_inc(ph_ready, 1)
                if v == 0:
                    pe.wait_ge(bias_ready, 1)
            pe.wait_ge(hid_ready, 2)
            for g in range(GROUPS):
                nc.tensor.matmul(pk[:, 0:P], w2[:, g, :], hid[:, g, :], start=(g == 0), stop=(g == 1))
            pe.wait_ge(hid_ready, 4)
            for g in range(GROUPS):
                mm = nc.tensor.matmul(pv[:, g * HD:(g + 1) * HD], hid[:, 2 + g, :], w2v[:], start=True, stop=True)
            mm.then_inc(pkv_ready, 1)

        @block.vector
        def _(dve):
            nc.vector.memset(hid[:, :, NCMP:P], 0.0).then_inc(hid_zero, 1)
            nc.vector.memset(s.kc[0][:], 0.0)
            nc.vector.memset(s.kc[1][:], 0.0).then_inc(cleared, 1)
            nc.vector.memset(s.kw[0][HD:P, :], 0.0)
            nc.vector.memset(s.kw[1][0:HD, :], 0.0)
            dve.wait_ge(small_in, 16 * 6)
            for v in range(2):
                dve.wait_ge(pb_ready, v + 1)
                nc.vector.tensor_tensor(bias[:, v:v + 1], pb[:, v:v + 1], b1[:, v:v + 1], ALU.add).then_inc(bias_ready, 1)
            dve.wait_ge(pkv_ready, 1)
            dve.wait_ge(cleared, 1)
            for g in range(GROUPS):
                rows = slice(g * HD, (g + 1) * HD)
                nc.vector.tensor_scalar(s.kc[g][rows, 0:NCMP], pk[rows, 0:NCMP], b2k[rows, :], None, ALU.add)
            nc.vector.tensor_tensor(s.vc[:], pv[:, 0:P], b2v[:], ALU.add)

        @block.scalar
        def _(act):
            act.wait_ge(hid_zero, 1)
            for v in range(2):
                act.wait_ge(bias_ready, v + 1)
                for g in range(GROUPS):
                    act.wait_ge(ph_ready, 2 * v + g + 1)
                    nc.scalar.activation(hid[:, 2 * v + g, 0:NCMP], ph[2 * v + g][:, 0:NCMP], ACT.Gelu_apprx_tanh,
                                         bias=bias[:, v:v + 1]).then_inc(hid_ready, 1)
            act.wait_ge(vsw_in, 16)
            nc.scalar.activation(s.gates[:], s.vsw[:, :, V_GATE:V_DIFF], ACT.Sigmoid)


def compressed_attention(nc, d, s):
    from concourse import mybir
    from contextlib import ExitStack

    fp32 = mybir.dt.float32
    ALU = mybir.AluOpType
    ACT = mybir.ActivationFunctionType
    steps = [(c, g) for c in range(NCH) for g in range(GROUPS)]
    NS = len(steps)
    with ExitStack() as ctx:
        qT = ctx.enter_context(nc.sbuf_tensor("a_qT", [P, T], fp32))
        slope = ctx.enter_context(nc.sbuf_tensor("a_slope", [P, GROUPS], fp32))
        dist = ctx.enter_context(nc.sbuf_tensor("a_dist", [P, NT, P], fp32))
        valid = ctx.enter_context(nc.sbuf_tensor("a_valid", [P, NT], fp32))
        bias = ctx.enter_context(nc.sbuf_tensor("a_bias", [P, GROUPS, NT, P], fp32))
        prob = ctx.enter_context(nc.sbuf_tensor("a_prob", [P, 3, 4, P], fp32))
        probT = ctx.enter_context(nc.sbuf_tensor("a_probT", [P, 2, 4, P], fp32))
        stat = ctx.enter_context(nc.sbuf_tensor("a_stat", [P, 3, 4, 4], fp32))
        pq = [ctx.enter_context(nc.psum_tensor(f"a_pq{k}", [P, 4, P], fp32)) for k in range(3)]
        pt = [ctx.enter_context(nc.psum_tensor(f"a_pt{k}", [P, 4, P], fp32)) for k in range(2)]
        po = [ctx.enter_context(nc.psum_tensor(f"a_po{k}", [P, 4, P], fp32)) for k in range(2)]
        names = ("q_in0", "q_in1", "q_in2", "q_in3", "slope_in", "bias_even", "bias_odd", "pq_ready", "max_done", "neg_ready", "exp_done", "rz_step", "prob_ready",
                 "pbar_added", "pt_ready", "probT_ready", "po_ready", "out_done", "const_in")
        m = {n: nc.alloc_semaphore("a_" + n) for n in names}
        slope_in, bias_even, bias_odd, pq_ready, max_done, neg_ready, exp_done, rz_step, prob_ready, \
            pbar_added, pt_ready, probT_ready, po_ready, out_done, const_in = (m[n] for n in names[NCH:])
        q_in = [m[n] for n in names[:NCH]]
        with nc.Block() as block:
            @block.sync
            def _(sp):
                sp.dma_start(dist[:], d["cmp_dist"]).then_inc(const_in, 16)
                sp.dma_start(valid[:], d["cmp_valid"]).then_inc(const_in, 16)
        with nc.Fori(0, PAIRS) as i:
            with nc.Block() as block:
                @block.sync
                def _(sp):
                    sp.dma_start(slope[:], d["nsa_slope"][i]).then_inc(slope_in, 16)
                    for c in range(NCH):
                        sp.dma_start(qT[:, c * 512:(c + 1) * 512], d["qkT"][i][:, c * 512:(c + 1) * 512]).then_inc(q_in[c], 16)
                    for c in range(NCH):
                        sp.wait_ge(q_in[c], 16)

                @block.gpsimd
                def _(pool):
                    pool.wait_ge(slope_in, 16)

                    def make_bias(n):
                        c, g = steps[n]
                        nc.gpsimd.tensor_scalar(bias[:, g, 4 * c:4 * c + 4, :], dist[:, 4 * c:4 * c + 4, :],
                                                slope[:, g:g + 1], None, ALU.mult).then_inc(bias_even, 1)

                    pool.wait_ge(const_in, 32)
                    make_bias(0)
                    make_bias(2)
                    for n, (c, g) in enumerate(steps):
                        if n % 2 == 0 and n + 4 < NS:
                            make_bias(n + 4)
                        pool.wait_ge(prob_ready, n + 1)
                        acc = s.pbar[:, g, 4 * c:4 * c + 4, :]
                        nc.gpsimd.tensor_tensor(acc, acc, prob[:, n % 3, :, :], ALU.add).then_inc(pbar_added, 1)

                @block.tensor
                def _(pe):
                    def scores(n):
                        c, g = steps[n]
                        pe.wait_ge(q_in[c], 16)
                        if n >= 3:
                            pe.wait_ge(max_done, 4 * (n - 2))
                        for j in range(4):
                            t = (4 * c + j) * P
                            mm = nc.tensor.matmul(pq[n % 3][:, j, :], qT[:, t:t + P], s.kc[g][:], start=True, stop=True)
                        mm.then_inc(pq_ready, 1)

                    def transposes(n):
                        pe.wait_ge(prob_ready, n + 1)
                        if n >= 2:
                            pe.wait_ge(probT_ready, n - 1)
                        for j in range(4):
                            mm = nc.tensor.transpose(pt[n % 2][:, j, :], prob[:, n % 3, j, :], s.ident[:])
                        mm.then_inc(pt_ready, 1)

                    def values(n):
                        pe.wait_ge(probT_ready, n + 1)
                        if n >= 2:
                            pe.wait_ge(out_done, n - 1)
                        for j in range(4):
                            mm = nc.tensor.matmul(po[n % 2][:, j, :], probT[:, n % 2, j, :], s.vc[:], start=True, stop=True)
                        mm.then_inc(po_ready, 1)

                    scores(0)
                    scores(1)
                    for n in range(NS + 1):
                        if n + 2 < NS:
                            scores(n + 2)
                        if n < NS:
                            transposes(n)
                        if n >= 1:
                            values(n - 1)

                @block.vector
                def _(dve):
                    def scaled(n):
                        c, g = steps[n]
                        dve.wait_ge(pq_ready, n + 1)
                        dve.wait_ge((bias_even, bias_odd)[n % 2], n // 2 + 1)
                        if n >= 3:
                            dve.wait_ge(pt_ready, n - 2)
                            dve.wait_ge(pbar_added, n - 2)
                        for j in range(4):
                            nc.vector.tensor_tensor_reduce(out=prob[:, n % 3, j, :], in0=pq[n % 3][:, j, :],
                                                           in1=bias[:, g, 4 * c + j, :], scale=HD ** -0.5, scalar=-3e38,
                                                           op0=ALU.add, op1=ALU.max, accum_out=stat[:, n % 3, 0, j:j + 1]).then_inc(max_done, 1)
                        dve.wait_ge(max_done, 4 * n + 4)
                        nc.vector.tensor_scalar(stat[:, n % 3, 1, :], stat[:, n % 3, 0, :], -1.0, None, ALU.mult).then_inc(neg_ready, 1)

                    def normalized(n):
                        c, g = steps[n]
                        dve.wait_ge(exp_done, 4 * n + 4)
                        nc.vector.reciprocal(stat[:, n % 3, 3, :], stat[:, n % 3, 2, :]).then_inc(rz_step, 1)
                        dve.wait_ge(rz_step, 2 * n + 1)
                        nc.vector.tensor_tensor(stat[:, n % 3, 0, :], stat[:, n % 3, 3, :], valid[:, 4 * c:4 * c + 4], ALU.mult).then_inc(rz_step, 1)
                        dve.wait_ge(rz_step, 2 * n + 2)
                        nc.vector.tensor_tensor(prob[:, n % 3, :, :], prob[:, n % 3, :, :],
                                                stat[:, n % 3, 0, :].unsqueeze(2).to_broadcast([P, 4, P]), ALU.mult).then_inc(prob_ready, 1)

                    def gated(n):
                        c, g = steps[n]
                        dve.wait_ge(po_ready, n + 1)
                        h = NSA_HEADS // GROUPS * g + i
                        gate = s.gates[:, 4 * c:4 * c + 4, :].rearrange("p t (h b) -> p t h b", b=3)[:, :, h, 0]
                        y = s.ya[:, 4 * c:4 * c + 4, :].rearrange("p t (h e) -> p t h e", e=HD)[:, :, h, :]
                        nc.vector.tensor_tensor(y, po[n % 2][:, :, g * HD:(g + 1) * HD],
                                                gate.unsqueeze(2).to_broadcast([P, 4, HD]), ALU.mult).then_inc(out_done, 1)

                    dve.wait_ge(const_in, 32)
                    scaled(0)
                    for n in range(NS + 2):
                        if n + 1 < NS:
                            scaled(n + 1)
                        if n < NS:
                            normalized(n)
                        if n >= 2:
                            gated(n - 2)

                @block.scalar
                def _(act):
                    def make_bias(n):
                        c, g = steps[n]
                        nc.scalar.activation(bias[:, g, 4 * c:4 * c + 4, :], dist[:, 4 * c:4 * c + 4, :], ACT.Copy,
                                             scale=slope[:, g:g + 1]).then_inc(bias_odd, 1)

                    act.wait_ge(slope_in, 16)
                    act.wait_ge(const_in, 32)
                    make_bias(1)
                    make_bias(3)
                    for n in range(NS + 1):
                        if n % 2 == 1 and n + 4 < NS:
                            make_bias(n + 4)
                        if n < NS:
                            act.wait_ge(neg_ready, n + 1)
                            for j in range(4):
                                nc.scalar.activation(prob[:, n % 3, j, :], prob[:, n % 3, j, :], ACT.Exp, bias=stat[:, n % 3, 1, j:j + 1],
                                                     accum_out=stat[:, n % 3, 2, j:j + 1]).then_inc(exp_done, 1)
                        if n >= 1:
                            act.wait_ge(pt_ready, n)
                            if n >= 3:
                                act.wait_ge(po_ready, n - 2)
                            nc.scalar.activation(probT[:, (n - 1) % 2, :, :], pt[(n - 1) % 2][:], ACT.Copy).then_inc(probT_ready, 1)
            clear_semaphores(nc, [m[n] for n in names if n != "const_in"])


def selection(nc, d, s):
    from concourse import mybir
    from contextlib import ExitStack

    fp32 = mybir.dt.float32
    ALU = mybir.AluOpType
    ACT = mybir.ActivationFunctionType
    with ExitStack() as ctx:
        overlap = ctx.enter_context(nc.sbuf_tensor("s_overlap", [P, NBLK], fp32))
        keep = ctx.enter_context(nc.sbuf_tensor("s_keep", [P, NT, NBLK], fp32))
        force = ctx.enter_context(nc.sbuf_tensor("s_force", [P, NT, NBLK], fp32))
        pT = ctx.enter_context(nc.sbuf_tensor("s_pT", [P, 2, 4, P], fp32))
        imp = ctx.enter_context(nc.sbuf_tensor("s_imp", [P, GROUPS, NT, NBLK], fp32))
        top = ctx.enter_context(nc.sbuf_tensor("s_top", [P, GROUPS, NT, SEL_TOPK], fp32))
        rows = ctx.enter_context(nc.sbuf_tensor("s_rows", [P, NT, P], fp32))
        pt = [ctx.enter_context(nc.psum_tensor(f"s_pt{k}", [P, 4, P], fp32)) for k in range(2)]
        pi = [ctx.enter_context(nc.psum_tensor(f"s_pi{g}", [P, NT, NBLK], fp32)) for g in range(GROUPS)]
        pm = [ctx.enter_context(nc.psum_tensor(f"s_pm{k}", [P, 512], fp32)) for k in range(4)]
        const_in = nc.alloc_semaphore("s_const_in")
        pt_ready = nc.alloc_semaphore("s_pt_ready")
        pT_ready = nc.alloc_semaphore("s_pT_ready")
        pi_ready = nc.alloc_semaphore("s_pi_ready")
        dve_step = nc.alloc_semaphore("s_dve_step")
        zeroed = nc.alloc_semaphore("s_zeroed")
        rows_ready = nc.alloc_semaphore("s_rows_ready")
        pm_ready = nc.alloc_semaphore("s_pm_ready")
        steps = [(g, c) for g in range(GROUPS) for c in range(NCH)]
        col = (HD, 0)
        block = ctx.enter_context(nc.Block())

        @block.sync
        def _(sp):
            sp.dma_start(overlap[:], d["overlap"]).then_inc(const_in, 16)
            sp.dma_start(keep[:], d["sel_keep"]).then_inc(const_in, 16)
            sp.dma_start(force[:], d["sel_force"]).then_inc(const_in, 16)

        @block.gpsimd
        def _(pool):
            nc.gpsimd.memset(rows[:], 0.0).then_inc(zeroed, 1)

        @block.tensor
        def _(pe):
            pe.wait_ge(const_in, 48)

            def importance(n):
                g, c = steps[n]
                pe.wait_ge(pT_ready, n + 1)
                for j in range(4):
                    mm = nc.tensor.matmul(pi[g][:, 4 * c + j, :], pT[:, n % 2, j, :], overlap[:], start=True, stop=True)
                mm.then_inc(pi_ready, 1)

            for n, (g, c) in enumerate(steps):
                if n >= 2:
                    pe.wait_ge(pT_ready, n - 1)
                for j in range(4):
                    mm = nc.tensor.transpose(pt[n % 2][:, j, :], s.pbar[:, g, 4 * c + j, :], s.ident[:])
                mm.then_inc(pt_ready, 1)
                if n >= 1:
                    importance(n - 1)
            importance(len(steps) - 1)
            pe.wait_ge(rows_ready, GROUPS)
            for c in range(NCH):
                for j in range(4):
                    mm = nc.tensor.transpose(pm[c][:, j * P:(j + 1) * P], rows[:, 4 * c + j, :], s.ident[:])
                mm.then_inc(pm_ready, 1)

        @block.scalar
        def _(act):
            for n in range(len(steps)):
                act.wait_ge(pt_ready, n + 1)
                if n >= 2:
                    act.wait_ge(pi_ready, n - 1)
                nc.scalar.activation(pT[:, n % 2, :, :], pt[n % 2][:], ACT.Copy).then_inc(pT_ready, 1)
            for c in range(NCH):
                act.wait_ge(pm_ready, c + 1)
                nc.scalar.activation(s.qs[0][HD:P, c * 512:(c + 1) * 512], pm[c][HD:P, :], ACT.Copy)

        @block.vector
        def _(dve):
            done = 0
            dve.wait_ge(const_in, 48)
            dve.wait_ge(zeroed, 1)
            for g in range(GROUPS):
                dve.wait_ge(pi_ready, NCH * (g + 1))
                nc.vector.tensor_tensor(imp[:, g], pi[g][:], keep[:], ALU.mult).then_inc(dve_step, 1)
                done += 1
                dve.wait_ge(dve_step, done)
                nc.vector.tensor_tensor(imp[:, g], imp[:, g], force[:], ALU.add).then_inc(dve_step, 1)
                done += 1
                dve.wait_ge(dve_step, done)
                for t in range(NT):
                    nc.vector.max(top[:, g, t, :], imp[:, g, t, :]).then_inc(dve_step, 1)
                done += NT
                dve.wait_ge(dve_step, done)
                for t in range(NT):
                    nc.vector.match_replace(imp[:, g, t, :], top[:, g, t, :], imp[:, g, t, :], NEG).then_inc(dve_step, 1)
                done += NT
                dve.wait_ge(dve_step, done)
                nc.vector.tensor_scalar(rows[:, :, col[g]:col[g] + NBLK], imp[:, g], NEG, NEG, ALU.not_equal, ALU.mult).then_inc(rows_ready, 1)
            for c in range(NCH):
                dve.wait_ge(pm_ready, c + 1)
                nc.vector.tensor_copy(s.qs[1][0:HD, c * 512:(c + 1) * 512], pm[c][0:HD, :])


def chunks_of(start, count):
    return [(k, min(512, start + count - k)) for k in range(start, start + count, 512)]


QUERY_ORDER = [3, 4, 8, 5, 12, 6, 15, 7, 14, 2, 13, 1, 11, 10, 0, 9]


def lagging(chunks_per_unit):
    due = []
    for n in chunks_per_unit:
        for _ in range(n):
            f = len(due)
            due.append(max(due[-1] if due else 0, f if n == 1 else f - 1, 0))
    return due


def sparse_attention(nc, d, s):
    from concourse import mybir
    from contextlib import ExitStack

    fp32 = mybir.dt.float32
    ALU = mybir.AluOpType
    ACT = mybir.ActivationFunctionType
    AX = mybir.AxisListType
    SELECTED, WINDOWED = 1, 2
    units, flat = [], []
    for t in QUERY_ORDER:
        for g in range(GROUPS):
            for branch in (SELECTED, WINDOWED):
                first = 0 if branch == SELECTED else max(0, t * P - WINDOW)
                cs = chunks_of(first, (t + 1) * P - first)
                units.append((t, g, branch, len(flat), cs))
                flat += [(len(units) - 1, k, n, c) for c, (k, n) in enumerate(cs)]
    NU, NF = len(units), len(flat)
    end = [u[3] + len(u[4]) for u in units]
    due = lagging([len(u[4]) for u in units])
    q_chunks = list(dict.fromkeys(t // 4 for t in QUERY_ORDER))
    opens = [next(u for u in range(len(units)) if units[u][0] // 4 == c) for c in range(NCH)]
    with ExitStack() as ctx:
        slope = ctx.enter_context(nc.sbuf_tensor("b_slope", [P, GROUPS], fp32))
        dist = ctx.enter_context(nc.sbuf_tensor("b_dist", [P, T], fp32))
        wdist = ctx.enter_context(nc.sbuf_tensor("b_wdist", [P, WINDOW + P], fp32))
        bias = [ctx.enter_context(nc.sbuf_tensor(f"b_bias{g}", [P, T], fp32)) for g in range(GROUPS)]
        wbias = [ctx.enter_context(nc.sbuf_tensor(f"b_wbias{g}", [P, WINDOW + P], fp32)) for g in range(GROUPS)]
        prob = [ctx.enter_context(nc.sbuf_tensor(f"b_prob{k}", [P, T], fp32)) for k in range(3)]
        probT = ctx.enter_context(nc.sbuf_tensor("b_probT", [P, 4, 4, P], fp32))
        stat = ctx.enter_context(nc.sbuf_tensor("b_stat", [P, 4, 8], fp32))
        pq = [ctx.enter_context(nc.psum_tensor(f"b_pq{k}", [P, 512], fp32)) for k in range(3)]
        pt = [ctx.enter_context(nc.psum_tensor(f"b_pt{k}", [P, 4, P], fp32)) for k in range(3)]
        po = [ctx.enter_context(nc.psum_tensor(f"b_po{k}", [P, 512], fp32)) for k in range(2)]
        names = ("q_in0", "q_in1", "q_in2", "q_in3", "slope_in", "bias_ready", "scores_ready", "scaled", "max_ready", "exp_done", "turned",
                 "act_copied", "dve_copied", "used", "inverted", "gate_ready", "out_done")
        m = {n: nc.alloc_semaphore("b_" + n) for n in names}
        q_in = [m[n] for n in names[:NCH]]
        slope_in, bias_ready, scores_ready, scaled, max_ready, exp_done, turned, \
            act_copied, dve_copied, used, inverted, gate_ready, out_done = (m[n] for n in names[NCH:])
        const_in = nc.alloc_semaphore("b_const_in")
        with nc.Block() as block:
            @block.sync
            def _(sp):
                sp.dma_start(dist[:], d["dist"]).then_inc(const_in, 16)
                sp.dma_start(wdist[:], d["win_dist"]).then_inc(const_in, 16)

        def copied(eng, f):
            eng.wait_ge((act_copied, dve_copied)[f % 2], f // 2 + 1)

        with nc.Fori(0, PAIRS) as i:
            with nc.Block() as block:
                @block.sync
                def _(sp):
                    sp.dma_start(slope[:], d["nsa_slope"][i]).then_inc(slope_in, 16)
                    for c in q_chunks:
                        for g in range(GROUPS):
                            at = slice(g * HD, (g + 1) * HD), slice(c * 512, (c + 1) * 512)
                            sp.dma_start(s.qs[g][at], d["qkT"][i][at]).then_inc(q_in[c], 16)
                    sp.wait_ge(slope_in, 16)

                @block.gpsimd
                def _(pool):
                    pool.wait_ge(slope_in, 16)
                    pool.wait_ge(const_in, 32)
                    for g in range(GROUPS):
                        nc.gpsimd.tensor_scalar(wbias[g][:], wdist[:], slope[:, g:g + 1], None, ALU.mult)
                        nc.gpsimd.tensor_scalar(bias[g][:, T - 512:T], dist[:, T - 512:T], slope[:, g:g + 1], None, ALU.mult).then_inc(bias_ready, 1)
                    for g in range(GROUPS):
                        nc.gpsimd.tensor_scalar(bias[g][:, 0:T - 512], dist[:, 0:T - 512], slope[:, g:g + 1], None, ALU.mult).then_inc(bias_ready, 1)

                    for u, (t, g, branch, _, _) in enumerate(units):
                        h = NSA_HEADS // GROUPS * g + i
                        gate = s.gates[:, t, :].rearrange("p (h b) -> p h b", b=3)[:, h, branch:branch + 1]
                        pool.wait_ge(inverted, u + 1)
                        nc.gpsimd.tensor_tensor(stat[:, u % 4, 6:7], gate, stat[:, u % 4, 7:8], ALU.mult).then_inc(gate_ready, 1)

                @block.tensor
                def _(pe):
                    def scores(u):
                        t, g, branch, f0, cs = units[u]
                        keys = s.ks[g] if branch == SELECTED else s.kw[g]
                        if opens[t // 4] == u:
                            pe.wait_ge(q_in[t // 4], 32)
                        for c, (k, n) in enumerate(cs):
                            f = f0 + c
                            if f >= 3:
                                pe.wait_ge(scaled, f - 2)
                            nc.tensor.matmul(pq[f % 3][:, 0:n], s.qs[g][:, t * P:(t + 1) * P], keys[:, k:k + n],
                                             start=True, stop=True).then_inc(scores_ready, 1)

                    def turn(f):
                        u, k, n, c = flat[f]
                        if c == 0:
                            pe.wait_ge(exp_done, u + 1)
                        if f >= 3:
                            copied(pe, f - 3)
                        row = c * 512
                        for j in range(n // P):
                            mm = nc.tensor.transpose(pt[f % 3][:, j, :], prob[u % 3][:, row + j * P:row + (j + 1) * P], s.ident[:])
                        mm.then_inc(turned, 1)

                    def values(f):
                        u, k, n, c = flat[f]
                        t, g, branch, f0, cs = units[u]
                        copied(pe, f)
                        if c == 0 and u >= 2:
                            pe.wait_ge(out_done, u - 1)
                        v0 = V_SEL if branch == SELECTED else V_WIN
                        for j in range(n // P):
                            mm = nc.tensor.matmul(po[u % 2][:, 0:P], probT[:, f % 4, j, :], s.vsw[:, k // P + j, v0:v0 + P],
                                                  start=(c == 0 and j == 0), stop=(f + 1 == end[u] and j == n // P - 1))
                        mm.then_inc(used, 1)

                    scores(0)
                    scores(1)
                    n_used = 0
                    for u in range(NU):
                        if u + 2 < NU:
                            scores(u + 2)
                        for f in range(units[u][3], end[u]):
                            turn(f)
                            for v in range(n_used, due[f]):
                                values(v)
                            n_used = due[f]
                    for v in range(n_used, NF):
                        values(v)

                @block.scalar
                def _(act):
                    def exponential(u):
                        n = sum(x for _, x in units[u][4])
                        act.wait_ge(max_ready, u + 1)
                        nc.scalar.activation(prob[u % 3][:, 0:n], prob[u % 3][:, 0:n], ACT.Exp, bias=stat[:, u % 4, 4:5],
                                             accum_out=stat[:, u % 4, 5:6]).then_inc(exp_done, 1)

                    exponential(0)
                    for u in range(NU):
                        if u + 1 < NU:
                            exponential(u + 1)
                        for f in range(units[u][3], end[u]):
                            if f % 2 == 0:
                                n = flat[f][2] // P
                                act.wait_ge(turned, f + 1)
                                if f >= 4:
                                    act.wait_ge(used, f - 3)
                                nc.scalar.activation(probT[:, f % 4, 0:n, :], pt[f % 3][:, 0:n, :], ACT.Copy).then_inc(act_copied, 1)

                @block.vector
                def _(dve):
                    def scale(u):
                        t, g, branch, f0, cs = units[u]
                        if u == 0 or u == 2:
                            dve.wait_ge(bias_ready, u // 2 + 1)
                        if u == 2 * GROUPS:
                            dve.wait_ge(bias_ready, 2 * GROUPS)
                        if u >= 3:
                            dve.wait_ge(turned, end[u - 3])
                        for c, (k, n) in enumerate(cs):
                            b = (bias[g][:, k + T - (t + 1) * P:k + T - (t + 1) * P + n] if branch == SELECTED
                                 else wbias[g][:, k + WINDOW - t * P:k + WINDOW - t * P + n])
                            dve.wait_ge(scores_ready, f0 + c + 1)
                            nc.vector.tensor_tensor_reduce(out=prob[u % 3][:, c * 512:c * 512 + n], in0=pq[(f0 + c) % 3][:, 0:n], in1=b,
                                                           scale=HD ** -0.5, scalar=-3e38, op0=ALU.add, op1=ALU.max,
                                                           accum_out=stat[:, u % 4, c:c + 1]).then_inc(scaled, 1)
                        dve.wait_ge(scaled, end[u])
                        nc.vector.tensor_reduce(stat[:, u % 4, 4:5], stat[:, u % 4, 0:len(cs)], AX.X, ALU.max, negate=True).then_inc(max_ready, 1)

                    def add_output(u):
                        t, g, branch, _, _ = units[u]
                        y = s.ya[:, t, :].rearrange("p (h e) -> p h e", e=HD)[:, NSA_HEADS // GROUPS * g + i, :]
                        dve.wait_ge(used, end[u])
                        dve.wait_ge(gate_ready, u + 1)
                        if u >= 1:
                            dve.wait_ge(out_done, u)
                        nc.vector.scalar_tensor_tensor(out=y, in0=po[u % 2][:, g * HD:(g + 1) * HD], scalar=stat[:, u % 4, 6:7],
                                                       in1=y, op0=ALU.mult, op1=ALU.add).then_inc(out_done, 1)

                    scale(0)
                    scale(1)
                    for u in range(NU):
                        if u + 2 < NU:
                            scale(u + 2)
                        dve.wait_ge(exp_done, u + 1)
                        nc.vector.reciprocal(stat[:, u % 4, 7:8], stat[:, u % 4, 5:6]).then_inc(inverted, 1)
                        fs = [f for f in range(units[u][3], end[u]) if f % 2 == 1]
                        for j, f in enumerate(fs):
                            n = flat[f][2] // P
                            dve.wait_ge(turned, f + 1)
                            if f >= 4:
                                dve.wait_ge(used, f - 3)
                            nc.vector.tensor_copy(probT[:, f % 4, 0:n, :], pt[f % 3][:, 0:n, :]).then_inc(dve_copied, 1)
                            if j == 0 and u >= 1:
                                add_output(u - 1)
                        if not fs and u >= 1:
                            add_output(u - 1)
                    add_output(NU - 1)
            clear_semaphores(nc, [m[n] for n in names])


def differential_attention(nc, d, s):
    from concourse import mybir
    from contextlib import ExitStack

    fp32 = mybir.dt.float32
    ALU = mybir.AluOpType
    ACT = mybir.ActivationFunctionType
    AX = mybir.AxisListType
    units, parts, flat = [], [], []
    for u, t in enumerate(QUERY_ORDER):
        cs = chunks_of(0, (t + 1) * P)
        units.append((len(parts), len(flat), cs, t))
        parts += [(u, m, k, n) for m in range(2) for k, n in cs]
        flat += [(u, k, n, c) for c, (k, n) in enumerate(cs)]
    NU, NF, RING = len(units), len(flat), 8
    p_end = [u[0] + 2 * len(u[2]) for u in units]
    f_end = [u[1] + len(u[2]) for u in units]
    due = lagging([len(u[2]) for u in units])
    opens = [next(u for u in range(NU) if units[u][3] // 4 >= c) for c in range(NCH)]
    with ExitStack() as ctx:
        q = ctx.enter_context(nc.sbuf_tensor("d_q", [P, T], fp32))
        keys = [ctx.enter_context(nc.sbuf_tensor(f"d_keys{m}", [P, T], fp32)) for m in range(2)]
        vals = ctx.enter_context(nc.sbuf_tensor("d_vals", [P, NT, P], fp32))
        slope = ctx.enter_context(nc.sbuf_tensor("d_slope", [P, 1], fp32))
        dist = ctx.enter_context(nc.sbuf_tensor("d_dist", [P, T], fp32))
        bias = ctx.enter_context(nc.sbuf_tensor("d_bias", [P, T], fp32))
        prob = [ctx.enter_context(nc.sbuf_tensor(f"d_prob{k}", [P, 2, T], fp32)) for k in range(4)]
        probT = ctx.enter_context(nc.sbuf_tensor("d_probT", [P, 4, 4, P], fp32))
        square = ctx.enter_context(nc.sbuf_tensor("d_square", [P, P], fp32))
        chunk_max = ctx.enter_context(nc.sbuf_tensor("d_chunk_max", [P, RING, 2, 4], fp32))
        stat = ctx.enter_context(nc.sbuf_tensor("d_stat", [P, RING, 8], fp32))
        ssq = ctx.enter_context(nc.sbuf_tensor("d_ssq", [P, NT], fp32))
        lam_in = ctx.enter_context(nc.sbuf_tensor("d_lam_in", [P, 4, HD], fp32))
        lam = ctx.enter_context(nc.sbuf_tensor("d_lam", [P, 8], fp32))
        pq = [ctx.enter_context(nc.psum_tensor(f"d_pq{k}", [P, 512], fp32)) for k in range(3)]
        pt = [ctx.enter_context(nc.psum_tensor(f"d_pt{k}", [P, 4, P], fp32)) for k in range(3)]
        po = [ctx.enter_context(nc.psum_tensor(f"d_po{k}", [P, 512], fp32)) for k in range(2)]
        names = ("q_in0", "q_in1", "q_in2", "q_in3", "slope_in", "bias_ready", "scores_ready", "scaled", "max_ready", "exp_done", "inverted", "ratio_ready",
                 "combined", "turned", "act_copied", "dve_copied", "used", "out_done", "squared")
        m_ = {n: nc.alloc_semaphore("d_" + n) for n in names}
        q_in = [m_[n] for n in names[:NCH]]
        slope_in, bias_ready, scores_ready, scaled, max_ready, exp_done, inverted, ratio_ready, \
            combined, turned, act_copied, dve_copied, used, out_done, squared = (m_[n] for n in names[NCH:])
        const_in = nc.alloc_semaphore("d_const_in")
        dist_in = nc.alloc_semaphore("d_dist_in")
        lam_step = nc.alloc_semaphore("d_lam_step")
        lam_exp = nc.alloc_semaphore("d_lam_exp")
        with nc.Block() as block:
            @block.sync
            def _(sp):
                sp.dma_start(lam_in[:], d["diff_lambda"]).then_inc(const_in, 16)
                sp.dma_start(dist[:], d["dist"]).then_inc(dist_in, 16)

            @block.vector
            def _(dve):
                nc.vector.memset(keys[0][HD:P, :], 0.0)
                nc.vector.memset(keys[1][0:HD, :], 0.0)
                dve.wait_ge(const_in, 16)
                for j in range(2):
                    nc.vector.tensor_tensor_reduce(out=lam_in[:, 2 * j, :], in0=lam_in[:, 2 * j, :], in1=lam_in[:, 2 * j + 1, :],
                                                   scale=1.0, scalar=0.0, op0=ALU.mult, op1=ALU.add,
                                                   accum_out=lam[:, j:j + 1]).then_inc(lam_step, 1)
                dve.wait_ge(lam_exp, 1)
                nc.vector.tensor_tensor(lam[:, 4:5], lam[:, 3:4], lam[:, 2:3], ALU.subtract).then_inc(lam_step, 1)
                dve.wait_ge(lam_step, 3)
                nc.vector.tensor_scalar(lam[:, 5:6], lam[:, 4:5], -LAM_INIT, None, ALU.add)

            @block.scalar
            def _(act):
                act.wait_ge(lam_step, 2)
                nc.scalar.activation(lam[:, 2:4], lam[:, 0:2], ACT.Exp).then_inc(lam_exp, 1)

        def copied(eng, f):
            eng.wait_ge((act_copied, dve_copied)[f % 2], f // 2 + 1)

        with nc.Fori(0, DIFF_HEADS) as i:
            with nc.Block() as block:
                @block.sync
                def _(sp):
                    sp.dma_start(slope[:], d["diff_slope"][i]).then_inc(slope_in, 16)
                    for c in range(NCH):
                        cols = slice(c * 512, (c + 1) * 512)
                        sp.dma_start(q[:, cols], d["qkT"][2 * i + T_DIFF][:, cols]).then_inc(q_in[c], 16)
                        for m in range(2):
                            at = slice(m * HD, (m + 1) * HD), cols
                            sp.dma_start(keys[m][at], d["qkT"][2 * i + T_DIFF + 1][at]).then_inc(q_in[c], 16)
                        v = d["vd"].rearrange("p t (h e) -> p t h e", e=P)[:, 4 * c:4 * c + 4, i, :]
                        sp.dma_start(vals[:, 4 * c:4 * c + 4, :], v).then_inc(q_in[c], 16)
                    sp.wait_ge(slope_in, 16)

                @block.gpsimd
                def _(pool):
                    pool.wait_ge(slope_in, 16)
                    pool.wait_ge(dist_in, 16)
                    for c in reversed(range(NCH)):
                        nc.gpsimd.tensor_scalar(bias[:, c * 512:(c + 1) * 512], dist[:, c * 512:(c + 1) * 512], slope[:, 0:1], None,
                                                ALU.mult).then_inc(bias_ready, 1)

                @block.tensor
                def _(pe):
                    def scores(u):
                        p0, _, cs, t = units[u]
                        for c in range(NCH):
                            if opens[c] == u:
                                pe.wait_ge(q_in[c], 64)
                        for p in range(p0, p_end[u]):
                            _, m, k, n = parts[p]
                            if p >= 3:
                                pe.wait_ge(scaled, p - 2)
                            nc.tensor.matmul(pq[p % 3][:, 0:n], q[:, t * P:(t + 1) * P], keys[m][:, k:k + n],
                                             start=True, stop=True).then_inc(scores_ready, 1)

                    def turn(f):
                        u, k, n, c = flat[f]
                        if c == 0:
                            pe.wait_ge(combined, u + 1)
                        if f >= 3:
                            copied(pe, f - 3)
                        for j in range(n // P):
                            mm = nc.tensor.transpose(pt[f % 3][:, j, :], prob[u % 4][:, 0, k + j * P:k + (j + 1) * P], s.ident[:])
                        mm.then_inc(turned, 1)

                    def values(f):
                        u, k, n, c = flat[f]
                        copied(pe, f)
                        if c == 0 and u >= 2:
                            pe.wait_ge(out_done, u - 1)
                            pe.wait_ge(squared, u - 1)
                        for j in range(n // P):
                            mm = nc.tensor.matmul(po[u % 2][:, 0:P], probT[:, f % 4, j, :], vals[:, k // P + j, :],
                                                  start=(c == 0 and j == 0), stop=(f + 1 == f_end[u] and j == n // P - 1))
                        mm.then_inc(used, 1)

                    for u in range(3):
                        scores(u)
                    n_used = 0
                    for u in range(NU):
                        if u + 3 < NU:
                            scores(u + 3)
                        for f in range(units[u][1], f_end[u]):
                            turn(f)
                            for v in range(n_used, due[f]):
                                values(v)
                            n_used = due[f]
                    for v in range(n_used, NF):
                        values(v)

                @block.scalar
                def _(act):
                    def exponential(u):
                        n = (units[u][3] + 1) * P
                        act.wait_ge(max_ready, u + 1)
                        for m in range(2):
                            nc.scalar.activation(prob[u % 4][:, m, 0:n], prob[u % 4][:, m, 0:n], ACT.Exp, bias=stat[:, u % RING, m:m + 1],
                                                 accum_out=stat[:, u % RING, 2 + m:3 + m]).then_inc(exp_done, 1)

                    def sum_squares(u):
                        act.wait_ge(used, f_end[u])
                        act.wait_ge(out_done, u + 1)
                        if u >= 1:
                            act.wait_ge(squared, u)
                        nc.scalar.activation(square[:], po[u % 2][:, 0:P], ACT.Square, scale=stat[:, u % RING, 4:5],
                                             accum_out=ssq[:, units[u][3]:units[u][3] + 1]).then_inc(squared, 1)

                    exponential(0)
                    exponential(1)
                    for u in range(NU):
                        if u + 2 < NU:
                            exponential(u + 2)
                        fs = [f for f in range(units[u][1], f_end[u]) if f % 2 == 0]
                        for j, f in enumerate(fs):
                            n = flat[f][2] // P
                            act.wait_ge(turned, f + 1)
                            if f >= 4:
                                act.wait_ge(used, f - 3)
                            nc.scalar.activation(probT[:, f % 4, 0:n, :], pt[f % 3][:, 0:n, :], ACT.Copy).then_inc(act_copied, 1)
                        if u >= 1:
                            sum_squares(u - 1)
                    sum_squares(NU - 1)

                @block.vector
                def _(dve):
                    def scale(u):
                        p0, _, cs, t = units[u]
                        for c in range(NCH):
                            if opens[c] == u:
                                dve.wait_ge(bias_ready, c + 1)
                        if u >= 4:
                            dve.wait_ge(turned, f_end[u - 4])
                        for p in range(p0, p_end[u]):
                            _, m, k, n = parts[p]
                            dve.wait_ge(scores_ready, p + 1)
                            nc.vector.tensor_tensor_reduce(out=prob[u % 4][:, m, k:k + n], in0=pq[p % 3][:, 0:n],
                                                           in1=bias[:, k + T - (t + 1) * P:k + T - (t + 1) * P + n],
                                                           scale=HD ** -0.5, scalar=-3e38, op0=ALU.add, op1=ALU.max,
                                                           accum_out=chunk_max[:, u % RING, m, k // 512:k // 512 + 1]).then_inc(scaled, 1)
                        dve.wait_ge(scaled, p_end[u])
                        nc.vector.tensor_reduce(stat[:, u % RING, 0:2], chunk_max[:, u % RING, :, 0:len(cs)], AX.X, ALU.max,
                                                negate=True).then_inc(max_ready, 1)

                    def combine(u):
                        n = (units[u][3] + 1) * P
                        dve.wait_ge(exp_done, 2 * u + 2)
                        nc.vector.reciprocal(stat[:, u % RING, 4:6], stat[:, u % RING, 2:4]).then_inc(inverted, 1)
                        dve.wait_ge(inverted, u + 1)
                        nc.vector.tensor_scalar(stat[:, u % RING, 6:7], stat[:, u % RING, 2:3], stat[:, u % RING, 5:6], lam[:, 5:6],
                                                ALU.mult, ALU.mult).then_inc(ratio_ready, 1)
                        dve.wait_ge(ratio_ready, u + 1)
                        nc.vector.scalar_tensor_tensor(out=prob[u % 4][:, 0, 0:n], in0=prob[u % 4][:, 1, 0:n], scalar=stat[:, u % RING, 6:7],
                                                       in1=prob[u % 4][:, 0, 0:n], op0=ALU.mult, op1=ALU.add).then_inc(combined, 1)

                    def output(u):
                        y = s.yb[:, units[u][3], :].rearrange("p (h e) -> p h e", e=P)[:, i, :]
                        dve.wait_ge(used, f_end[u])
                        nc.vector.tensor_scalar(y, po[u % 2][:, 0:P], stat[:, u % RING, 4:5], None, ALU.mult).then_inc(out_done, 1)

                    for u in range(3):
                        scale(u)
                    combine(0)
                    for u in range(NU):
                        if u + 3 < NU:
                            scale(u + 3)
                        if u + 1 < NU:
                            combine(u + 1)
                        for j, f in enumerate(f for f in range(units[u][1], f_end[u]) if f % 2 == 1):
                            n = flat[f][2] // P
                            dve.wait_ge(turned, f + 1)
                            if f >= 4:
                                dve.wait_ge(used, f - 3)
                            nc.vector.tensor_copy(probT[:, f % 4, 0:n, :], pt[f % 3][:, 0:n, :]).then_inc(dve_copied, 1)
                        if u >= 1:
                            output(u - 1)
                    output(NU - 1)
                    dve.wait_ge(squared, NU)
                    nc.vector.tensor_copy(s.ssq[:, :, i], ssq[:])
            clear_semaphores(nc, [m_[n] for n in names])


def transpose_branches(nc, d, s, xnT):
    from concourse import mybir
    from contextlib import ExitStack

    fp32 = mybir.dt.float32
    ALU = mybir.AluOpType
    ACT = mybir.ActivationFunctionType
    steps = [(k, c) for c in range(NCH) for k in range(4)]
    NS = len(steps)
    with ExitStack() as ctx:
        var = ctx.enter_context(nc.sbuf_tensor("t_var", [P, NT, DIFF_HEADS], fp32))
        rstd = ctx.enter_context(nc.sbuf_tensor("t_rstd", [P, NT, DIFF_HEADS], fp32))
        gain = ctx.enter_context(nc.sbuf_tensor("t_gain", [P, 1], fp32))
        pa = [ctx.enter_context(nc.psum_tensor(f"t_pa{k}", [P, 4, P], fp32)) for k in range(3)]
        pb = [ctx.enter_context(nc.psum_tensor(f"t_pb{k}", [P, 4, P], fp32)) for k in range(3)]
        gain_in = nc.alloc_semaphore("t_gain_in")
        s.xnt_in = nc.alloc_semaphore("t_xnt_in")
        var_ready = nc.alloc_semaphore("t_var_ready")
        rstd_ready = nc.alloc_semaphore("t_rstd_ready")
        normed = nc.alloc_semaphore("t_normed")
        a_turned = nc.alloc_semaphore("t_a_turned")
        b_turned = nc.alloc_semaphore("t_b_turned")
        a_copied = [nc.alloc_semaphore(f"t_a_copied{k}") for k in range(2)]
        b_copied = [nc.alloc_semaphore(f"t_b_copied{k}") for k in range(2)]
        gain_ready = nc.alloc_semaphore("t_gain_ready")
        block = ctx.enter_context(nc.Block())

        @block.sync
        def _(sp):
            sp.dma_start(gain[:], d["subln_g"]).then_inc(gain_in, 16)
            for dt in range(DT):
                sp.dma_start(xnT[:, dt, :], d["xnT"][:, dt, :]).then_inc(s.xnt_in, 16)

        @block.gpsimd
        def _(pool):
            pool.wait_ge(var_ready, 1)
            nc.gpsimd.tensor_tensor(rstd[:], var[:], s.half[:, 0:1].unsqueeze(2).to_broadcast([P, NT, DIFF_HEADS]), ALU.pow).then_inc(rstd_ready, 1)

        @block.vector
        def _(dve):
            nc.vector.tensor_scalar(var[:], s.ssq[:], 1.0 / P, SUBLN_EPS, ALU.mult, ALU.add).then_inc(var_ready, 1)
            dve.wait_ge(rstd_ready, 1)
            dve.wait_ge(gain_in, 16)
            nc.vector.tensor_scalar(gain[:], gain[:], 1.0 - LAM_INIT, None, ALU.mult).then_inc(gain_ready, 1)
            dve.wait_ge(gain_ready, 1)
            for t in range(NT):
                y = s.yb[:, t, :].rearrange("p (h e) -> p h e", e=P)
                nc.vector.tensor_tensor(y, y, rstd[:, t, :].unsqueeze(2).to_broadcast([P, DIFF_HEADS, P]), ALU.mult).then_inc(normed, 1)
            for n, (k, c) in enumerate(steps):
                if n % 2 == 1:
                    dve.wait_ge(b_turned, n + 1)
                    nc.vector.tensor_scalar(s.ybT[:, k, c * 512:(c + 1) * 512], pb[n % 3][:].rearrange("p a b -> p (a b)"), gain[:, 0:1],
                                            None, ALU.mult).then_inc(b_copied[1], 1)

        @block.scalar
        def _(act):
            for n, (k, c) in enumerate(steps):
                act.wait_ge(a_turned, n + 1)
                nc.scalar.activation(s.yaT[:, k, c * 512:(c + 1) * 512], pa[n % 3][:].rearrange("p a b -> p (a b)"), ACT.Copy).then_inc(a_copied[n % 2], 1)
            act.wait_ge(gain_ready, 1)
            for n, (k, c) in enumerate(steps):
                if n % 2 == 0:
                    act.wait_ge(b_turned, n + 1)
                    nc.scalar.activation(s.ybT[:, k, c * 512:(c + 1) * 512], pb[n % 3][:].rearrange("p a b -> p (a b)"), ACT.Copy,
                                         scale=gain[:, 0:1]).then_inc(b_copied[0], 1)

        @block.tensor
        def _(pe):
            for y, banks, turned, copied in ((s.ya, pa, a_turned, a_copied), (s.yb, pb, b_turned, b_copied)):
                for n, (k, c) in enumerate(steps):
                    if y is s.yb:
                        pe.wait_ge(normed, 4 * c + 4)
                    if n >= 3:
                        pe.wait_ge(copied[(n - 3) % 2], (n - 3) // 2 + 1)
                    for j in range(4):
                        mm = nc.tensor.transpose(banks[n % 3][:, j, :], y[:, 4 * c + j, k * P:(k + 1) * P], s.ident[:])
                    mm.then_inc(turned, 1)


def merge_branches(nc, d, s, xnT):
    from concourse import mybir
    from contextlib import ExitStack

    fp32 = mybir.dt.float32
    ALU = mybir.AluOpType
    ACT = mybir.ActivationFunctionType
    NW = 2 * DT + 8
    with ExitStack() as ctx:
        a_room, b_room = (y[:].rearrange("p t c -> p (t c)") for y in (s.ya, s.yb))
        w = a_room[:, 0:2 * NW * P].rearrange("p (b k c) -> p b k c", b=2, c=P)
        sig = a_room[:, 2 * NW * P:2 * NW * P + 4 * 512].rearrange("p (b k c) -> p b k c", b=2, c=512)
        stage = b_room[:, 0:2 * T].rearrange("p (b c) -> p b c", b=2)
        ps = [[ctx.enter_context(nc.psum_tensor(f"m_ps{b}{k}", [P, 512], fp32)) for k in range(4)] for b in range(2)]
        w_in = [nc.alloc_semaphore(f"m_w_in{b}") for b in range(2)]
        gates_ready = nc.alloc_semaphore("m_gates_ready")
        all_ready = nc.alloc_semaphore("m_all_ready")
        sig_ready = nc.alloc_semaphore("m_sig_ready")
        gated = nc.alloc_semaphore("m_gated")
        summed = nc.alloc_semaphore("m_summed")
        stored = [nc.alloc_semaphore(f"m_stored{b}") for b in range(2)]
        sp_step = nc.alloc_semaphore("m_sp_step")
        block = ctx.enter_context(nc.Block())

        @block.sync
        def _(sp):
            for b in range(2):
                sp.sem_inc(stored[b], 16)
                sp.dma_start(w[:, b, :, :], d["w_merge"][b]).then_inc(w_in[b], 16)
            with sp.Fori(0, DT // 2) as i:
                for b in range(2):
                    sp.wait_ge(all_ready, 8 * i + 4 * b + 4)
                    sp.sem_inc(sp_step, 1)
                    sp.dma_start(w[:, b, :, :], d["w_merge"][2 * i + b + 2]).then_inc(w_in[b], 16)
                    sp.wait_ge(summed, 8 * i + 4 * b + 6)
                    sp.sem_inc(sp_step, 1)
                    sp.dma_start(d["mergedT"][2 * i + b], stage[:, b, :]).then_inc(stored[b], 16)
            for b in range(2):
                sp.wait_ge(stored[b], 16 * (DT // 2 + 1))
                sp.wait_ge(w_in[b], 16 * (DT // 2 + 1))

        @block.tensor
        def _(pe):
            pe.wait_ge(s.xnt_in, 16 * DT)
            with pe.Fori(0, DT // 2) as i:
                for b in range(2):
                    pe.wait_ge(w_in[b], 16 * i + 16)
                    for c in range(NCH):
                        toks = slice(c * 512, (c + 1) * 512)
                        bank = ps[c % 2]
                        pe.wait_ge(gated, 8 * i + 4 * b + c + 1)
                        for k in range(2):
                            for dt in range(DT):
                                mm = nc.tensor.matmul(bank[k][:], w[:, b, DT * k + dt, :], xnT[:, dt, toks], start=(dt == 0), stop=(dt == DT - 1))
                        mm.then_inc(gates_ready, 1)
                        for k, y in ((0, s.yaT), (1, s.ybT)):
                            for kt in range(4):
                                mm = nc.tensor.matmul(bank[2 + k][:], w[:, b, 2 * DT + 4 * k + kt, :], y[:, kt, toks], start=(kt == 0), stop=(kt == 3))
                        mm.then_inc(all_ready, 1)

        @block.scalar
        def _(act):
            with act.Fori(0, DT // 2) as i:
                for b in range(2):
                    for c in range(NCH):
                        n = 8 * i + 4 * b + c
                        act.wait_ge(gates_ready, n + 1)
                        act.wait_ge(summed, n + 1)
                        for k in range(2):
                            nc.scalar.activation(sig[:, c % 2, k, :], ps[c % 2][k][:], ACT.Sigmoid).then_inc(sig_ready, 1)

        @block.vector
        def _(dve):
            dve.sem_inc(gated, 2)
            with dve.Fori(0, DT // 2) as i:
                for b in range(2):
                    for c in range(NCH):
                        n = 8 * i + 4 * b + c
                        dve.wait_ge(all_ready, n + 1)
                        dve.wait_ge(sig_ready, 2 * n + 2)
                        nc.vector.tensor_tensor(sig[:, c % 2, 0, :], sig[:, c % 2, 0, :], ps[c % 2][2][:], ALU.mult)
                        nc.vector.tensor_tensor(sig[:, c % 2, 1, :], sig[:, c % 2, 1, :], ps[c % 2][3][:], ALU.mult).then_inc(gated, 1)

        @block.gpsimd
        def _(pool):
            pool.sem_inc(summed, 2)
            with pool.Fori(0, DT // 2) as i:
                for b in range(2):
                    pool.wait_ge(stored[b], 16 * i + 16)
                    pool.sem_inc(sp_step, 1)
                    for c in range(NCH):
                        pool.wait_ge(gated, 8 * i + 4 * b + c + 3)
                        pool.sem_inc(sp_step, 1)
                        nc.gpsimd.tensor_tensor(stage[:, b, c * 512:(c + 1) * 512], sig[:, c % 2, 0, :], sig[:, c % 2, 1, :], ALU.add).then_inc(summed, 1)


def project_and_route(nc, d, s):
    from concourse import mybir
    from contextlib import ExitStack

    fp32 = mybir.dt.float32
    ALU = mybir.AluOpType
    ACT = mybir.ActivationFunctionType
    NR = NG + NG * NE
    with ExitStack() as ctx:
        sem = ctx.enter_context(phase_semaphores(nc))
        w = ctx.enter_context(nc.sbuf_tensor("o_w", [P, DT, D], fp32))
        wr = ctx.enter_context(nc.sbuf_tensor("o_wr", [P, DT, NR], fp32))
        br = ctx.enter_context(nc.sbuf_tensor("o_br", [P, NR], fp32))
        gain = ctx.enter_context(nc.sbuf_tensor("o_gain", [P, D], fp32))
        mT = ctx.enter_context(nc.sbuf_tensor("o_mT", [P, 2, DT, P], fp32))
        x = ctx.enter_context(nc.sbuf_tensor("o_x", [P, 2, D], fp32))
        h = ctx.enter_context(nc.sbuf_tensor("o_h", [P, 2, D], fp32))
        square = ctx.enter_context(nc.sbuf_tensor("o_square", [P, D], fp32))
        xg = ctx.enter_context(nc.sbuf_tensor("o_xg", [P, 2, D], fp32))
        xgT = ctx.enter_context(nc.sbuf_tensor("o_xgT", [P, DT, P], fp32))
        stat = ctx.enter_context(nc.sbuf_tensor("o_stat", [P, 2, 4], fp32))
        ps = [[ctx.enter_context(nc.psum_tensor(f"o_ps{b}{k}", [P, 512], fp32)) for k in range(2)] for b in range(2)]
        pt = [ctx.enter_context(nc.psum_tensor(f"o_pt{k}", [P, 4, P], fp32)) for k in range(2)]
        pr = ctx.enter_context(nc.psum_tensor("o_pr", [P, 512], fp32))
        w_in = [sem(f"o_w_in{k}") for k in range(DT)]
        mT_in = [sem(f"o_mT_in{b}") for b in range(2)]
        x_in = [sem(f"o_x_in{b}") for b in range(2)]
        h_stored = [sem(f"o_h_stored{b}") for b in range(2)]
        xg_stored = [sem(f"o_xg_stored{b}") for b in range(2)]
        const_in, out_ready, out_taken, h_ready, ss_ready, var_ready, rstd_ready, scaled, xg_ready, turned, xgT_ready, \
            logits_ready, logits_taken, step = (sem("o_" + n) for n in (
                "const_in", "out_ready", "out_taken", "h_ready", "ss_ready", "var_ready", "rstd_ready", "scaled", "xg_ready",
                "turned", "xgT_ready", "logits_ready", "logits_taken", "step"))
        m_t = d["mergedT"].rearrange("k p (n t) -> n p k t", t=P)
        x_t, h_t, xg_t = (a.rearrange("(n p) c -> n p c", p=P) for a in (d["x"], d["h"], d["xg"]))
        block = ctx.enter_context(nc.Block())

        def lagged(ahead, behind, loop, behind_first=False):
            def both(one, other):
                for step, i, b in ((behind, *other), (ahead, *one)) if behind_first else ((ahead, *one), (behind, *other)):
                    step(i, b)

            ahead(0, 0)
            with loop as i:
                both((i, 1), (i, 0))
                both((i + 1, 0), (i, 1))
            ahead(NT // 2 - 1, 1)
            behind(NT // 2 - 1, 0)
            behind(NT // 2 - 1, 1)

        @block.sync
        def _(sp):
            for b in range(2):
                sp.sem_inc(h_stored[b], 16)
                sp.sem_inc(xg_stored[b], 16)
                sp.dma_start(mT[:, b, :, :], m_t[b]).then_inc(mT_in[b], 16)
                sp.dma_start(x[:, b, :], x_t[b]).then_inc(x_in[b], 16)
                for dt in range(b * DT // 2, (b + 1) * DT // 2):
                    sp.dma_start(w[:, dt, :], d["w_out"][:, dt, :]).then_inc(w_in[dt], 16)
            for o, i in ((gain, d["norm2_row"]), (wr, d["w_router"]), (br, d["b_router"])):
                sp.dma_start(o[:], i).then_inc(const_in, 16)

            def store(i, b):
                sp.wait_ge(h_ready, 2 * i + b + 1)
                sp.sem_inc(step, 1)
                sp.dma_start(h_t[2 * i + b], h[:, b, :]).then_inc(h_stored[b], 16)
                sp.wait_ge(xg_ready, 2 * i + b + 1)
                sp.sem_inc(step, 1)
                sp.dma_start(xg_t[2 * i + b], xg[:, b, :]).then_inc(xg_stored[b], 16)

            with sp.Fori(0, NT // 2 - 1) as i:
                for b in range(2):
                    sp.wait_ge(h_ready, 2 * i + b + 1)
                    sp.sem_inc(step, 1)
                    sp.dma_start(mT[:, b, :, :], m_t[2 * i + b + 2]).then_inc(mT_in[b], 16)
                    sp.dma_start(x[:, b, :], x_t[2 * i + b + 2]).then_inc(x_in[b], 16)
                    store(i, b)
            for g in range(2):
                load_experts(sp, d, s, g)
            for b in range(2):
                store(NT // 2 - 1, b)
            for b in range(2):
                sp.wait_ge(h_stored[b], 16 * (NT // 2 + 1))
                sp.wait_ge(xg_stored[b], 16 * (NT // 2 + 1))

        @block.gpsimd
        def _(pool):
            with pool.Fori(0, NT // 2) as i:
                for b in range(2):
                    pool.wait_ge(var_ready, 2 * i + b + 1)
                    pool.sem_inc(step, 1)
                    nc.gpsimd.tensor_tensor(stat[:, b, 2:3], stat[:, b, 1:2], s.half[:, 0:1], ALU.pow).then_inc(rstd_ready, 1)

        @block.tensor
        def _(pe):
            def product(i, b):
                pe.wait_ge(mT_in[b], 16 * i + 16)
                pe.wait_ge(out_taken, 2 * i + b + 1)
                for dt in range(DT):
                    if isinstance(i, int) and i == 0:
                        pe.wait_ge(w_in[dt], 16)
                    for k in range(2):
                        mm = nc.tensor.matmul(ps[b][k][:], mT[:, b, dt, :], w[:, dt, k * 512:(k + 1) * 512], start=(dt == 0), stop=(dt == DT - 1))
                mm.then_inc(out_ready, 1)

            def turn(i, b):
                pe.wait_ge(xg_ready, 2 * i + b + 1)
                for dt in range(DT):
                    mm = nc.tensor.transpose(pt[dt // 4][:, dt % 4, :], xg[:, b, dt * P:(dt + 1) * P], s.ident[:])
                mm.then_inc(turned, 1)

            def route(i, b):
                pe.wait_ge(xgT_ready, 2 * i + b + 1)
                pe.wait_ge(logits_taken, 2 * i + b + 1)
                for dt in range(DT):
                    mm = nc.tensor.matmul(pr[:, 0:NR], xgT[:, dt, :], wr[:, dt, :], start=(dt == 0), stop=(dt == DT - 1))
                mm.then_inc(logits_ready, 1)

            product(0, 0)
            product(0, 1)
            turn(0, 0)
            product(1, 0)
            route(0, 0)
            turn(0, 1)
            with pe.Fori(1, NT // 2 - 1) as i:
                product(i, 1)
                route(i - 1, 1)
                turn(i, 0)
                product(i + 1, 0)
                route(i, 0)
                turn(i, 1)
            last = NT // 2 - 1
            product(last, 1)
            route(last - 1, 1)
            turn(last, 0)
            route(last, 0)
            turn(last, 1)
            route(last, 1)

        @block.scalar
        def _(act):
            def normalize(i, b):
                act.wait_ge(h_ready, 2 * i + b + 1)
                nc.scalar.activation(square[:], h[:, b, :], ACT.Square, accum_out=stat[:, b, 0:1]).then_inc(ss_ready, 1)
                act.wait_ge(xg_stored[b], 16 * i + 16)
                act.wait_ge(rstd_ready, 2 * i + b + 1)
                nc.scalar.activation(xg[:, b, :], h[:, b, :], ACT.Copy, scale=stat[:, b, 2:3]).then_inc(scaled, 1)

            def copy(i, b):
                act.wait_ge(turned, 2 * i + b + 1)
                for k in range(2):
                    cp = nc.scalar.activation(xgT[:, 4 * k:4 * k + 4, :], pt[k][:], ACT.Copy)
                cp.then_inc(xgT_ready, 1)

            lagged(normalize, copy, act.Fori(0, NT // 2 - 1), behind_first=True)

        @block.vector
        def _(dve):
            def add(i, b):
                dve.wait_ge(x_in[b], 16 * i + 16)
                dve.wait_ge(out_ready, 2 * i + b + 1)
                dve.wait_ge(h_stored[b], 16 * i + 16)
                for k in range(2):
                    cols = slice(k * 512, (k + 1) * 512)
                    op = nc.vector.tensor_tensor(h[:, b, cols], ps[b][k][:], x[:, b, cols], ALU.add)
                op.then_inc(h_ready, 1)
                dve.wait_ge(h_ready, 2 * i + b + 1)
                dve.sem_inc(out_taken, 1)
                dve.wait_ge(ss_ready, 2 * i + b + 1)
                nc.vector.tensor_scalar(stat[:, b, 1:2], stat[:, b, 0:1], 1.0 / D, RMS_EPS, ALU.mult, ALU.add).then_inc(var_ready, 1)
                dve.wait_ge(scaled, 2 * i + b + 1)
                nc.vector.tensor_tensor(xg[:, b, :], xg[:, b, :], gain[:], ALU.mult).then_inc(xg_ready, 1)

            def logits(i, b):
                dve.wait_ge(logits_ready, 2 * i + b + 1)
                nc.vector.tensor_tensor(s.logits[:, 2 * i + b, :], pr[:, 0:NR], br[:], ALU.add).then_inc(logits_taken, 1)

            dve.sem_inc(out_taken, 2)
            dve.sem_inc(logits_taken, 1)
            dve.wait_ge(const_in, 48)
            lagged(add, logits, dve.Fori(0, NT // 2 - 1))


def load_experts(eng, d, s, g):
    for k in range(2):
        eng.dma_start(s.wgu[g % 2][:, k], d["w_gu"][g, :, k]).then_inc(s.gu_in[g][k], 16)
    eng.dma_start(s.wd[g % 2][:], d["w_down"][g]).then_inc(s.d_in[g], 16)


def choose_experts(nc, d, s):
    from concourse import mybir
    from contextlib import ExitStack

    fp32, i32 = mybir.dt.float32, mybir.dt.int32
    ALU = mybir.AluOpType
    ACT = mybir.ActivationFunctionType
    AX = mybir.AxisListType
    with ExitStack() as ctx:
        sem = ctx.enter_context(phase_semaphores(nc))
        def sb(name, shape):
            return ctx.enter_context(nc.sbuf_tensor("r_" + name, shape, fp32))

        before, ones, zeros = sb("before", [P, P]), sb("ones", [P, P]), sb("zeros", [P, D])
        tokens, steps_of = sb("tokens", [P, NT]), sb("steps_of", [P, NG, NT])
        best, exps, total = sb("best", [P, NT, 1]), sb("exps", [P, NT, NG]), sb("total", [P, NT, 1])
        eq, taken, group = sb("eq", [P, NT, NG]), sb("taken", [P, NT, 1]), sb("group", [P, NT, NG])
        rank, picked = sb("rank", [P, NE]), sb("picked", [P, NT, NG, NE])
        elog, first, second = sb("elog", [P, NT, NE]), sb("first", [P, NT, NE]), sb("second", [P, NT, NE])
        v1, v2, w1, w2, gw = (sb(n, [P, NT, 1]) for n in ("v1", "v2", "w1", "w2", "gw"))
        ahead, other = sb("ahead", [P, NT + 1, NG]), sb("other", [P, NT + 1, NG])
        tiles, base = sb("tiles", [P, NG]), sb("base", [P, NG + 1])
        more, place, slotf = sb("more", [P, NG, NT]), sb("place", [P, NT, NG]), sb("slotf", [P, NT])
        row = sb("row", [P, NT, ROW])
        pc = ctx.enter_context(nc.psum_tensor("r_pc", [P, NT, NG], fp32))
        pn = ctx.enter_context(nc.psum_tensor("r_pn", [P, NT, NG], fp32))
        const_in, chain, exp_ready, group_ready, counted, slots_ready, zeroed, cleared, y_cleared, scattered = (
            sem("r_" + n) for n in ("const_in", "chain", "exp_ready", "group_ready", "counted", "slots_ready",
                                                   "zeroed", "cleared", "y_cleared", "scattered"))
        block = ctx.enter_context(nc.Block())
        glog = s.logits[:, :, 0:NG]
        xlog = s.logits[:, :, NG:NG + NG * NE].rearrange("p t (g e) -> p t g e", e=NE)

        @block.sync
        def _(sp):
            sp.dma_start(before[:], d["before"]).then_inc(const_in, 16)
            sp.dma_start(tokens[:], d["tokens"]).then_inc(const_in, 16)
            sp.dma_start(steps_of[:], d["steps_of"]).then_inc(const_in, 16)
            sp.wait_ge(zeroed, 1)
            sp.dma_start(d["table"].rearrange("(p a) r -> p (a r)", p=P), zeros[:, 0:NSLOT // P * ROW]).then_inc(cleared, 16)
            y_t = d["y"].rearrange("(n p) c -> n p c", p=P)
            for n in range(NT, NSLOT // P):
                sp.dma_start(y_t[n], zeros[:]).then_inc(y_cleared, 16)
            sp.wait_ge(y_cleared, 16 * (NSLOT // P - NT))

        @block.tensor
        def _(pe):
            pe.wait_ge(const_in, 48)
            pe.wait_ge(zeroed, 1)
            pe.wait_ge(group_ready, 1)
            nc.tensor.matmul(pc[:].rearrange("p t g -> p (t g)"), before[:], group[:].rearrange("p t g -> p (t g)"), start=True, stop=True)
            nc.tensor.matmul(pn[:].rearrange("p t g -> p (t g)"), ones[:], group[:].rearrange("p t g -> p (t g)"), start=True, stop=True).then_inc(counted, 1)

        @block.scalar
        def _(act):
            act.wait_ge(exp_ready, 1)
            nc.scalar.activation(exps[:], exps[:], ACT.Exp).then_inc(exp_ready, 1)
            act.wait_ge(exp_ready, 3)
            nc.scalar.activation(w2[:], w2[:], ACT.Exp).then_inc(exp_ready, 1)

        @block.gpsimd
        def _(pool):
            import concourse.bass as bass
            pool.wait_ge(slots_ready, 1)
            pool.wait_ge(cleared, 16)
            for t in range(NT):
                nc.gpsimd.indirect_dma_start(d["table"], bass.IndirectOffsetOnAxis(ap=s.slot[:, t:t + 1], axis=0), row[:, t, :], None).then_inc(scattered, 16)
            pool.wait_ge(scattered, 16 * NT)

        @block.vector
        def _(dve):
            count = [0]

            def link(op):
                count[0] += 1
                op.then_inc(chain, 1)
                dve.wait_ge(chain, count[0])

            def wide(x, n):
                return x[:].to_broadcast([P, NT, n])

            def first_of(out, equal):
                link(nc.vector.tensor_tensor(out[:], equal[:], rank[:].unsqueeze(1).to_broadcast([P, NT, NE]), ALU.mult))
                link(nc.vector.tensor_reduce(taken[:], out[:], AX.X, ALU.max))
                link(nc.vector.tensor_tensor(out[:], out[:], wide(taken, NE), ALU.is_equal))

            nc.vector.memset(ones[:], 1.0)
            nc.vector.memset(row[:], 0.0)
            nc.vector.memset(ahead[:, 0, :], 0.0)
            nc.vector.memset(base[:], 0.0)
            for j in range(NE):
                nc.vector.memset(rank[:, j:j + 1], float(NE - j))
            link(nc.vector.memset(zeros[:], 0.0))
            dve.sem_inc(zeroed, 1)
            dve.wait_ge(const_in, 48)
            link(nc.vector.tensor_reduce(best[:], glog, AX.X, ALU.max))
            link(nc.vector.tensor_tensor(exps[:], glog, wide(best, NG), ALU.subtract))
            dve.sem_inc(exp_ready, 1)
            link(nc.vector.tensor_tensor(eq[:], glog, wide(best, NG), ALU.is_equal))
            first_of(group, eq)
            dve.sem_inc(group_ready, 1)
            link(nc.vector.tensor_tensor(picked[:], xlog, group[:].unsqueeze(3).to_broadcast([P, NT, NG, NE]), ALU.mult))
            link(nc.vector.tensor_tensor(elog[:], picked[:, :, 0, :], picked[:, :, 1, :], ALU.add))
            link(nc.vector.tensor_tensor(elog[:], elog[:], picked[:, :, 2, :], ALU.add))
            link(nc.vector.tensor_tensor(elog[:], elog[:], picked[:, :, 3, :], ALU.add))
            link(nc.vector.tensor_reduce(v1[:], elog[:], AX.X, ALU.max))
            link(nc.vector.tensor_tensor(eq[:], elog[:], wide(v1, NE), ALU.is_equal))
            first_of(first, eq)
            link(nc.vector.scalar_tensor_tensor(out=elog[:], in0=first[:], scalar=-3e38, in1=elog[:], op0=ALU.mult, op1=ALU.add))
            link(nc.vector.tensor_reduce(v2[:], elog[:], AX.X, ALU.max))
            link(nc.vector.tensor_tensor(eq[:], elog[:], wide(v2, NE), ALU.is_equal))
            first_of(second, eq)
            link(nc.vector.tensor_tensor(w2[:], v2[:], v1[:], ALU.subtract))
            dve.wait_ge(exp_ready, 2)
            dve.sem_inc(exp_ready, 1)
            link(nc.vector.tensor_reduce(total[:], exps[:], AX.X, ALU.add))
            link(nc.vector.reciprocal(gw[:], total[:]))
            dve.wait_ge(exp_ready, 4)
            link(nc.vector.tensor_scalar(total[:], w2[:], 1.0, None, ALU.add))
            link(nc.vector.reciprocal(w1[:], total[:]))
            link(nc.vector.tensor_tensor(w2[:], w2[:], w1[:], ALU.mult))
            link(nc.vector.tensor_tensor(w2[:], w2[:], gw[:], ALU.mult))
            link(nc.vector.tensor_tensor(w1[:], w1[:], gw[:], ALU.mult))
            link(nc.vector.tensor_tensor(first[:], first[:], wide(w1, NE), ALU.mult))
            link(nc.vector.tensor_tensor(second[:], second[:], wide(w2, NE), ALU.mult))
            link(nc.vector.tensor_tensor(row[:, :, 1:1 + NE], first[:], second[:], ALU.add))
            link(nc.vector.tensor_copy(row[:, :, 0:1].bitcast(i32), tokens[:].unsqueeze(2)))
            dve.wait_ge(counted, 1)
            link(nc.vector.tensor_copy(ahead[:, 1:NT + 1, :], pn[:]))
            wide_sum, step = (ahead, other), 1
            while step < NT:
                a, b = wide_sum
                nc.vector.tensor_copy(b[:, 1:step + 1, :], a[:, 1:step + 1, :])
                link(nc.vector.tensor_tensor(b[:, step + 1:NT + 1, :], a[:, step + 1:NT + 1, :], a[:, 1:NT + 1 - step, :], ALU.add))
                wide_sum, step = (b, a), 2 * step
            assert wide_sum[0] is ahead
            link(nc.vector.tensor_tensor(more[:], ahead[:, NT, :].unsqueeze(2).to_broadcast([P, NG, NT]), steps_of[:], ALU.is_gt))
            link(nc.vector.tensor_reduce(tiles[:], more[:], AX.X, ALU.add))
            link(nc.vector.tensor_scalar(tiles[:], tiles[:], 1.0, None, ALU.max))
            for g in range(NG):
                link(nc.vector.tensor_tensor(base[:, g + 1:g + 2], base[:, g:g + 1], tiles[:, g:g + 1], ALU.add))
            nc.vector.tensor_copy(s.first[:], base[:])
            link(nc.vector.tensor_tensor(place[:], ahead[:, 0:NT, :], pc[:], ALU.add))
            link(nc.vector.tensor_scalar(base[:], base[:], float(P), None, ALU.mult))
            link(nc.vector.tensor_tensor(place[:], place[:], base[:, 0:NG].unsqueeze(1).to_broadcast([P, NT, NG]), ALU.add))
            link(nc.vector.tensor_tensor(place[:], place[:], group[:], ALU.mult))
            link(nc.vector.tensor_reduce(slotf[:], place[:], AX.X, ALU.add))
            link(nc.vector.tensor_copy(s.slot[:], slotf[:]))
            dve.sem_inc(slots_ready, 1)


def experts(nc, d, s):
    import concourse.bass as bass
    from concourse import mybir
    from contextlib import ExitStack

    fp32, i32 = mybir.dt.float32, mybir.dt.int32
    ALU = mybir.AluOpType
    ACT = mybir.ActivationFunctionType
    MAXT = NSLOT // P
    with ExitStack() as ctx:
        def sb(name, shape, dt=fp32):
            return ctx.enter_context(nc.sbuf_tensor("e_" + name, shape, dt))

        def register_ends(eng):
            return [eng.value_load(s.first[0:1, g:g + 1], min_val=min(g, 1) * g, max_val=MAXT - 1) for g in range(NG + 1)]

        wgu, wd = s.wgu, s.wd
        table = sb("table", [P, MAXT, ROW])
        index = sb("index", [P, 1], i32)
        x, xT = sb("x", [P, D]), sb("xT", [P, DT, P])
        act_out, hid, hidT = sb("act", [P, 2, 2 * FF]), sb("hid", [P, 2, 2, FF]), sb("hidT", [P, 2, 2, P])
        y = sb("y", [P, D])
        pgu = [ctx.enter_context(nc.psum_tensor(f"e_pgu{k}", [P, 4, FF], fp32)) for k in range(2)]
        px = [ctx.enter_context(nc.psum_tensor(f"e_px{k}", [P, 4, P], fp32)) for k in range(2)]
        ph = [ctx.enter_context(nc.psum_tensor(f"e_ph{k}", [P, 2, P], fp32)) for k in range(2)]
        py = [ctx.enter_context(nc.psum_tensor(f"e_py{k}", [P, 512], fp32)) for k in range(2)]
        h_in, table_in, index_ready, gathered, x_turned, xT_ready, gu_ready, silu_done, hid_ready, hid_turned, hidT_ready, y_ready, \
            y_copied, y_stored, group_done, step = (nc.alloc_semaphore("e_" + n) for n in (
                "h_in", "table_in", "index_ready", "gathered", "x_turned", "xT_ready", "gu_ready", "silu_done", "hid_ready", "hid_turned",
                "hidT_ready", "y_ready", "y_copied", "y_stored", "group_done", "step"))
        y_t = d["y"].rearrange("(n p) c -> n p c", p=P)
        block = ctx.enter_context(nc.Block())

        @block.sync
        def _(sp):
            sp.dma_start(table[:], d["table"].rearrange("(n p) r -> p n r", p=P)).then_inc(table_in, 16)

            for g in range(2, NG):
                sp.wait_ge(group_done, g - 1)
                load_experts(sp, d, s, g)
            h_t = d["h"].rearrange("(n p) c -> p n c", p=P)
            for k in range(4):
                sp.wait_ge(x_turned, NT - 4 + k)
                sp.dma_start(s.h[:, 4 * k:4 * k + 4, :], h_t[:, 4 * k:4 * k + 4, :]).then_inc(h_in, 16)
            sp.wait_ge(h_in, 16 * 4)

        @block.gpsimd
        def _(pool):
            ends = register_ends(pool)
            pool.wait_ge(table_in, 16)

            def fetch(n):
                nc.gpsimd.tensor_copy(index[:], table[:, n, 0:1].bitcast(i32)).then_inc(index_ready, 1)
                pool.wait_ge(index_ready, n + 1)
                pool.sem_inc(step, 1)
                nc.gpsimd.indirect_dma_start(x[:], None, d["xg"], bass.IndirectOffsetOnAxis(ap=index[:], axis=0)).then_inc(gathered, 16)

            fetch(0)
            with pool.Fori(1, ends[NG] + 1) as n:
                pool.wait_ge(x_turned, n)
                pool.sem_inc(step, 1)
                fetch(n)

        @block.tensor
        def _(pe):
            ends = register_ends(pe)

            def turn_x(n):
                pe.wait_ge(gathered, 16 * n + 16)
                for dt in range(DT):
                    mm = nc.tensor.transpose(px[dt // 4][:, dt % 4, :], x[:, dt * P:(dt + 1) * P], s.ident[:])
                mm.then_inc(x_turned, 1)

            turn_x(0)
            for g in range(NG):
                for q in (*s.gu_in[g], s.d_in[g]):
                    pe.wait_ge(q, 16)
                with pe.Fori(ends[g], ends[g + 1]) as n:
                    pe.wait_ge(xT_ready, n + 1)
                    for k in range(2):
                        for dt in range(DT):
                            mm = nc.tensor.matmul(pgu[k][:].rearrange("p a b -> p (a b)"), xT[:, dt, :], wgu[g % 2][:, k, dt, :],
                                                  start=(dt == 0), stop=(dt == DT - 1))
                        mm.then_inc(gu_ready, 1)
                    turn_x(n + 1)
                    for k in range(2):
                        pe.wait_ge(hid_ready, 2 * n + k + 1)
                        for e in range(2):
                            mm = nc.tensor.transpose(ph[k][:, e, :], hid[:, k, e, :], s.ident[:])
                        mm.then_inc(hid_turned, 1)
                    pe.wait_ge(y_copied, 2 * n + 2)
                    for k in range(2):
                        pe.wait_ge(hidT_ready, 2 * n + k + 1)
                        for e in range(2):
                            for c in range(2):
                                mm = nc.tensor.matmul(py[c][:], hidT[:, k, e, :], wd[g % 2][:, 2 * k + e, c * 512:(c + 1) * 512],
                                                      start=(k == 0 and e == 0), stop=(k == 1 and e == 1))
                    mm.then_inc(y_ready, 1)
                pe.wait_ge(y_ready, ends[g + 1])
                pe.sem_inc(group_done, 1)

        @block.scalar
        def _(act):
            ends = register_ends(act)
            with act.Fori(0, ends[NG]) as n:
                for k in range(2):
                    act.wait_ge(gu_ready, 2 * n + k + 1)
                    nc.scalar.activation(act_out[:, k, :], pgu[k][:, 0:2, :].rearrange("p a b -> p (a b)"), ACT.Silu).then_inc(silu_done, 1)
                for k in range(2):
                    act.wait_ge(hid_turned, 2 * n + k + 1)
                    nc.scalar.activation(hidT[:, k, :, :], ph[k][:], ACT.Copy).then_inc(hidT_ready, 1)
                act.wait_ge(y_ready, n + 1)
                act.wait_ge(y_stored, 16 * n + 16)
                nc.scalar.activation(y[:, 0:512], py[0][:], ACT.Copy).then_inc(y_copied, 1)
                act.wait_ge(y_copied, 2 * n + 4)
                act.dma_start(y_t[n], y[:]).then_inc(y_stored, 16)
            act.wait_ge(y_stored, 16 * ends[NG] + 16)
            act.sem_inc(step, 1)

        @block.vector
        def _(dve):
            ends = register_ends(dve)
            dve.sem_inc(y_copied, 2)
            dve.sem_inc(y_stored, 16)

            def copy_x(n):
                dve.wait_ge(x_turned, n + 1)
                for k in range(2):
                    cp = nc.vector.tensor_copy(xT[:, 4 * k:4 * k + 4, :], px[k][:])
                cp.then_inc(xT_ready, 1)

            dve.wait_ge(table_in, 16)
            copy_x(0)
            with dve.Fori(0, ends[NG]) as n:
                for k in range(2):
                    dve.wait_ge(silu_done, 2 * n + k + 1)
                    for e in range(2):
                        op = nc.vector.scalar_tensor_tensor(out=hid[:, k, e, :], in0=act_out[:, k, e * FF:(e + 1) * FF],
                                                            scalar=table[:, n, 1 + 2 * k + e:2 + 2 * k + e], in1=pgu[k][:, 2 + e, :],
                                                            op0=ALU.mult, op1=ALU.mult)
                    op.then_inc(hid_ready, 1)
                copy_x(n + 1)
                dve.wait_ge(y_ready, n + 1)
                dve.wait_ge(y_stored, 16 * n + 16)
                nc.vector.tensor_copy(y[:, 512:D], py[1][:]).then_inc(y_copied, 1)


def finish(nc, d, s, out):
    import concourse.bass as bass
    from concourse import mybir
    from contextlib import ExitStack

    fp32, i32 = mybir.dt.float32, mybir.dt.int32
    ALU = mybir.AluOpType
    ACT = mybir.ActivationFunctionType
    NB = 4
    with ExitStack() as ctx:
        h = s.h
        y = ctx.enter_context(nc.sbuf_tensor("f_y", [P, NB, D], fp32))
        square = ctx.enter_context(nc.sbuf_tensor("f_square", [P, D], fp32))
        gain = ctx.enter_context(nc.sbuf_tensor("f_gain", [P, D], fp32))
        stat = ctx.enter_context(nc.sbuf_tensor("f_stat", [P, NT, 4], fp32))
        gain_in = nc.alloc_semaphore("f_gain_in")
        y_in = [nc.alloc_semaphore(f"f_y_in{b}") for b in range(NB)]
        stored = nc.alloc_semaphore("f_stored")
        added, ss_ready, var_ready, rstd_ready, done = (nc.alloc_semaphore("f_" + n) for n in (
            "added", "ss_ready", "var_ready", "rstd_ready", "done"))
        out_t = out[0].rearrange("(n p) c -> n p c", p=P)
        block = ctx.enter_context(nc.Block())

        @block.sync
        def _(sp):
            sp.dma_start(gain[:], d["final_row"]).then_inc(gain_in, 16)

        @block.gpsimd
        def _(pool):
            def fetch(t):
                if t >= NB:
                    pool.wait_ge(added, t - NB + 1)
                nc.gpsimd.indirect_dma_start(y[:, t % NB, :], None, d["y"], bass.IndirectOffsetOnAxis(ap=s.slot[:, t:t + 1], axis=0)).then_inc(y_in[t % NB], 16)

            for t in range(NB - 1):
                fetch(t)
            for t in range(NT):
                if t + NB - 1 < NT:
                    fetch(t + NB - 1)
                pool.wait_ge(var_ready, t + 1)
                nc.gpsimd.tensor_tensor(stat[:, t, 2:3], stat[:, t, 1:2], s.half[:, 0:1], ALU.pow).then_inc(rstd_ready, 1)

        @block.scalar
        def _(act):
            def store(t):
                act.wait_ge(done, t + 1)
                act.dma_start(out_t[t], h[:, t, :]).then_inc(stored, 16)

            for t in range(NT):
                act.wait_ge(added, t + 1)
                if t >= 1:
                    act.wait_ge(ss_ready, t)
                nc.scalar.activation(square[:], h[:, t, :], ACT.Square, accum_out=stat[:, t, 0:1]).then_inc(ss_ready, 1)
                if t >= 2:
                    store(t - 2)
            store(NT - 2)
            store(NT - 1)
            act.wait_ge(stored, 16 * NT)

        @block.vector
        def _(dve):
            def add(t):
                dve.wait_ge(y_in[t % NB], 16 * (t // NB + 1))
                nc.vector.tensor_tensor(h[:, t, :], h[:, t, :], y[:, t % NB, :], ALU.add).then_inc(added, 1)

            def normalize(t):
                dve.wait_ge(rstd_ready, t + 1)
                nc.vector.scalar_tensor_tensor(out=h[:, t, :], in0=h[:, t, :], scalar=stat[:, t, 2:3], in1=gain[:],
                                               op0=ALU.mult, op1=ALU.mult).then_inc(done, 1)

            dve.wait_ge(gain_in, 16)
            add(0)
            for t in range(NT):
                if t + 1 < NT:
                    add(t + 1)
                dve.wait_ge(ss_ready, t + 1)
                nc.vector.tensor_scalar(stat[:, t, 1:2], stat[:, t, 0:1], 1.0 / D, RMS_EPS, ALU.mult, ALU.add).then_inc(var_ready, 1)
                if t >= 1:
                    normalize(t - 1)
            normalize(NT - 1)


class OnChip:
    pass


def program(nc, d, out):
    from concourse import mybir
    from contextlib import ExitStack

    fp32 = mybir.dt.float32
    d["qkT"] = nc.dram_tensor("qkT", [T_GATE, P, T], fp32, kind="Internal").ap()
    d["vsw"] = nc.dram_tensor("vsw_spill", [P, NT, V_DIFF], fp32, kind="Internal").ap()
    d["vd"] = nc.dram_tensor("vd_spill", [P, NT, DIFF_HEADS * P], fp32, kind="Internal").ap()
    d["mergedT"] = nc.dram_tensor("mergedT", [DT, P, T], fp32, kind="Internal").ap()
    d["xnT"] = nc.dram_tensor("xnT_spill", [P, DT, T], fp32, kind="Internal").ap()
    d["h"] = nc.dram_tensor("h", [T, D], fp32, kind="Internal").ap()
    d["xg"] = nc.dram_tensor("xg", [T, D], fp32, kind="Internal").ap()
    d["y"] = nc.dram_tensor("y", [NSLOT, D], fp32, kind="Internal").ap()
    d["table"] = nc.dram_tensor("table", [NSLOT, ROW], fp32, kind="Internal").ap()
    with ExitStack() as ctx:
        def sb(scope, name, shape, dt=fp32):
            return scope.enter_context(nc.sbuf_tensor(name, shape, dt))

        s = OnChip()
        s.ident = sb(ctx, "ident", [P, P])
        s.half = sb(ctx, "half", [P, 1])
        const_in = nc.alloc_semaphore("const_in")
        with nc.Block() as block:
            @block.sync
            def _(sp):
                sp.dma_start(s.ident[:], d["ident"]).then_inc(const_in, 16)
                sp.wait_ge(const_in, 16)

            @block.vector
            def _(dve):
                nc.vector.memset(s.half[:], -0.5)
        with ExitStack() as early:
            xnT = sb(early, "xnT", [P, DT, T])
            vsw = sb(early, "vsw_early", [P, NT, V_DIFF])
            vd = sb(early, "vd_early", [P, NT, DIFF_HEADS * P])
            norm_and_v_projection(nc, d["x"], d["wv"], d["g1"], s.ident, s.half, xnT, vsw, vd)
            t_projection(nc, d["wt"], xnT, d["qkT"], [(d["vsw"], vsw[:]), (d["vd"], vd[:]), (d["xnT"], xnT[:])])
        with ExitStack() as attention:
            s.ya = sb(attention, "ya", [P, NT, NSA_HEADS * HD])
            s.yb = sb(attention, "yb", [P, NT, DIFF_HEADS * P])
            s.ssq = sb(attention, "ssq", [P, NT, DIFF_HEADS])
            with ExitStack() as nsa:
                s.vsw = sb(nsa, "vsw", [P, NT, V_DIFF])
                s.ks = [sb(nsa, f"ks{g}", [P, T]) for g in range(GROUPS)]
                s.kw = [sb(nsa, f"kw{g}", [P, T]) for g in range(GROUPS)]
                s.qs = [sb(nsa, f"qs{g}", [P, T]) for g in range(GROUPS)]
                s.gates = sb(nsa, "gates", [P, NT, 3 * NSA_HEADS])
                with ExitStack() as cmp:
                    s.kc = [sb(cmp, f"kc{g}", [P, P]) for g in range(GROUPS)]
                    s.vc = sb(cmp, "vc", [P, P])
                    s.pbar = sb(cmp, "pbar", [P, GROUPS, NT, P])
                    compress(nc, d, s)
                    compressed_attention(nc, d, s)
                    selection(nc, d, s)
                sparse_attention(nc, d, s)
            differential_attention(nc, d, s)
            with ExitStack() as merge:
                xnT = sb(merge, "xnT_again", [P, DT, T])
                s.yaT = sb(merge, "yaT", [P, 4, T])
                s.ybT = sb(merge, "ybT", [P, 4, T])
                transpose_branches(nc, d, s, xnT)
                merge_branches(nc, d, s, xnT)
        s.logits = sb(ctx, "logits", [P, NT, NG + NG * NE])
        s.slot = sb(ctx, "slot", [P, NT], mybir.dt.int32)
        s.first = sb(ctx, "first", [P, NG + 1], mybir.dt.int32)
        s.wgu = [sb(ctx, f"wgu{b}", [P, 2, DT, 4 * FF]) for b in range(2)]
        s.wd = [sb(ctx, f"wd{b}", [P, NE, D]) for b in range(2)]
        s.gu_in = [[nc.alloc_semaphore(f"e_gu_in{g}{k}") for k in range(2)] for g in range(NG)]
        s.d_in = [nc.alloc_semaphore(f"e_d_in{g}") for g in range(NG)]
        project_and_route(nc, d, s)
        choose_experts(nc, d, s)
        s.h = sb(ctx, "h_again", [P, NT, D])
        experts(nc, d, s)
        finish(nc, d, s, out)


def lay_out(inputs):
    f = lambda n: np.ascontiguousarray(inputs[n])
    w_in = f("w_in")[0]
    cuts = np.cumsum([512] + [128] * 6 + [24, 512, 512, 512, D, D])
    nq, kc, vc, ks, vs, kw, vw, ngate, dq, dk, dv, ga, gb = np.split(w_in, cuts[:-1], axis=1)
    tiles = [np.concatenate([nq[:, i * HD:(i + 1) * HD], nq[:, (i + PAIRS) * HD:(i + PAIRS + 1) * HD]], 1) for i in range(PAIRS)]
    tiles += [kc, vc, ks, kw]
    tiled = lambda a: a.reshape(-1, P, a.shape[1]).transpose(1, 0, 2)
    for h in range(DIFF_HEADS):
        tiles += [dq[:, h * P:(h + 1) * P], dk[:, h * P:(h + 1) * P]]
    tiles += tiles[:2]
    wt = np.stack([tiled(t) for t in tiles])
    wv = np.concatenate([vs, vw, ngate, dv], 1).reshape(DT, P, VCOLS).transpose(1, 0, 2)
    col = lambda a: np.ascontiguousarray(a.reshape(DT, P).T)
    r = {"x": f("x")[0], "wt": np.ascontiguousarray(wt), "wv": np.ascontiguousarray(wv), "g1": col(f("norm1_g")[0])}
    wm = np.concatenate([tiled(ga), tiled(gb), tiled(f("w_branch_a")[0]), tiled(f("w_branch_b")[0])], 1)
    wm = wm.reshape(P, 2 * DT + 8, DT, P).transpose(2, 0, 1, 3)
    r["w_merge"] = np.concatenate([wm, wm[:2]])
    r["subln_g"] = f("diff_subln_g")[0][:, None].copy()
    r["diff_lambda"] = np.ascontiguousarray(np.broadcast_to(f("diff_lambda")[0], (P, 4, HD)))
    row = lambda n: np.ascontiguousarray(np.broadcast_to(f(n).reshape(1, -1), (P, D)))
    r["w_out"] = np.ascontiguousarray(tiled(f("w_out")[0]))
    r["norm2_row"], r["final_row"] = row("norm2_g"), row("final_norm_g")
    r["w_router"] = np.ascontiguousarray(tiled(np.concatenate([f("router_grp_w")[0], f("router_exp_w")[0].reshape(D, -1)], 1)))
    br = np.concatenate([f("router_grp_b")[0], f("router_exp_b")[0].reshape(-1)])
    r["b_router"] = np.ascontiguousarray(np.broadcast_to(br, (P, br.size)))
    wg = np.stack([f("exp_w_gate")[0], f("exp_w_up")[0]])
    wg = wg.reshape(2, NG, 2, 2, DT, P, FF).transpose(1, 5, 2, 4, 0, 3, 6)
    r["w_gu"] = np.ascontiguousarray(wg.reshape(NG, P, 2, DT, 4 * FF))
    r["w_down"] = np.ascontiguousarray(f("exp_w_down")[0].reshape(NG, NE, FF, D).transpose(0, 2, 1, 3))
    r["before"] = (np.arange(P)[:, None] < np.arange(P)[None, :]).astype(np.float32)
    r["tokens"] = (np.arange(NT)[None, :] * P + np.arange(P)[:, None]).astype(np.float32)
    r["steps_of"] = np.ascontiguousarray(np.broadcast_to((np.arange(NT) * P).astype(np.float32), (P, NG, NT)))
    nj = CMP_BLOCK // 2
    r["cmp_pe"] = np.ascontiguousarray(f("cmp_pe")[0].reshape(2, nj, P).transpose(2, 0, 1))
    r["cmp_w1"] = np.ascontiguousarray(f("cmp_w1")[0].reshape(2, nj, P, CMP_HIDDEN).transpose(0, 2, 1, 3))
    r["cmp_b1"] = np.ascontiguousarray(f("cmp_b1")[0].T)
    w2, b2 = f("cmp_w2")[0], f("cmp_b2")[0]
    w2k = np.zeros((P, GROUPS, P), np.float32)
    for g in range(GROUPS):
        w2k[:, g, g * HD:(g + 1) * HD] = w2[0]
    r["cmp_w2k"], r["cmp_w2v"] = w2k, np.ascontiguousarray(w2[1])
    r["cmp_b2k"] = np.concatenate([b2[0], b2[0]])[:, None].copy()
    r["cmp_b2v"] = np.ascontiguousarray(np.broadcast_to(np.concatenate([b2[1], b2[1]]), (P, P)))
    q = np.arange(P)[:, None]
    neg = np.float32(NEG)
    slopes = (2.0 ** (-8.0 * np.arange(1, N_ALIBI + 1) / N_ALIBI)).astype(np.float32) * np.float32(HD ** 0.5)
    r["ident"] = np.eye(P, dtype=np.float32)
    r["nsa_slope"] = np.ascontiguousarray(np.broadcast_to(slopes[:NSA_HEADS].reshape(GROUPS, PAIRS).T[:, None, :], (PAIRS, P, GROUPS)))
    k = np.arange(T)[None, :] - (T - P) - q
    r["diff_slope"] = np.ascontiguousarray(np.broadcast_to(slopes[NSA_HEADS:, None, None], (DIFF_HEADS, P, 1)))
    r["dist"] = np.where(k <= 0, k, neg).astype(np.float32)
    k = np.arange(WINDOW + P)[None, :] - WINDOW - q
    r["win_dist"] = np.where((k <= 0) & (k > -WINDOW), k, neg).astype(np.float32)
    t = np.arange(NT)[None, :] * P + q
    c = np.arange(P)
    k = (c * CMP_STRIDE + CMP_BLOCK - 1)[None, None, :] - t[:, :, None]
    r["cmp_dist"] = np.where((k <= 0) & (c < NCMP), k, neg).astype(np.float32)
    r["cmp_valid"] = (t >= CMP_BLOCK - 1).astype(np.float32)
    c0, s0 = c[:, None] * CMP_STRIDE, np.arange(NBLK)[None, :] * SEL_BLOCK
    ov = np.maximum(0, np.minimum(c0 + CMP_BLOCK, s0 + SEL_BLOCK) - np.maximum(c0, s0)) / CMP_BLOCK
    r["overlap"] = np.where(c[:, None] < NCMP, ov, 0).astype(np.float32)
    b, cur = np.arange(NBLK)[None, None, :], (t // SEL_BLOCK)[:, :, None]
    forced, future = (b == 0) | (b == cur) | (b == cur - 1), b * SEL_BLOCK > t[:, :, None]
    r["sel_keep"] = (~forced & ~future).astype(np.float32)
    r["sel_force"] = np.where(future, -1.0, np.where(forced, FORCED, 0.0)).astype(np.float32)
    r["blk_ind"] = (np.arange(HD)[:, None] == np.arange(T)[None, :] // SEL_BLOCK).astype(np.float32)
    return r


def kernel(**inputs):
    import concourse.bacc as bacc
    from concourse import mybir
    from concourse.bass_utils import run_bass_kernel_spmd as launch

    nc = bacc.Bacc("TRN2", target_bir_lowering=False, num_devices=1)
    arrays = lay_out(inputs)
    d = {k: nc.dram_tensor(f"in_{k}", a.shape, mybir.dt.from_np(a.dtype), kind="ExternalInput").ap() for k, a in arrays.items()}
    out = nc.dram_tensor("out_0", (1, T, D), mybir.dt.float32, kind="ExternalOutput").ap()
    program(nc, d, out)
    r = launch(nc, [{f"in_{k}": a for k, a in arrays.items()}], core_ids=[0])
    return r.results[0]["out_0"]
```
